# Optimizing a Trainium2 kernel written in Bass

```python
import jax, jax.numpy as jnp
from jax import lax
import numpy as np
import math

D_MODEL = 1024
BATCH = 1
SEQ = 512
DEPTH = 2

GRID_W = 64
CTX_LEN = 256
HEAD_DIM = 64
ATTN_DIM = D_MODEL // 2
N_Q_HEADS = ATTN_DIM // HEAD_DIM
N_KV_HEADS = N_Q_HEADS // 4
Q_PER_KV = N_Q_HEADS // N_KV_HEADS
KV_DIM = N_KV_HEADS * HEAD_DIM
GMLP_DIM = D_MODEL - ATTN_DIM
GMLP_GROUP_DIM = 128
N_GMLP_GROUPS = GMLP_DIM // GMLP_GROUP_DIM
CHUNK = 128
MIX_DIM = ATTN_DIM + GMLP_DIM
IN_DIM = ATTN_DIM + 2 * KV_DIM + 2 * GMLP_DIM
FF_DIM = 4 * D_MODEL
Q_BLOCK = 128
ROPE_THETA = 10000.0
EPS = 1e-6
N_MOD = 6


def rmsnorm(x, g):
    xf = x.astype(jnp.float32)
    y = xf * lax.rsqrt(jnp.mean(xf * xf, axis=-1, keepdims=True) + EPS)
    return (y * g.astype(jnp.float32)).astype(x.dtype)

def group_layernorm(v, g):
    vf = v.astype(jnp.float32)
    mu = jnp.mean(vf, axis=-1, keepdims=True)
    var = jnp.mean(jnp.square(vf - mu), axis=-1, keepdims=True)
    return ((vf - mu) * lax.rsqrt(var + EPS) * g.astype(jnp.float32)).astype(v.dtype)

def modulation(cond, w_mod, b_mod):
    m = jax.nn.silu(cond) @ w_mod + b_mod
    return m.reshape(m.shape[:-1] + (N_MOD, D_MODEL))

def modulate(h, shift, scale):
    return h * (1 + scale) + shift

def axial_rope_tables(n_lat):
    rows = n_lat // GRID_W
    row = jnp.repeat(jnp.arange(rows, dtype=jnp.float32), GRID_W)
    col = jnp.tile(jnp.arange(GRID_W, dtype=jnp.float32), rows)
    n_freq = HEAD_DIM // 4
    inv_freq = ROPE_THETA ** (-jnp.arange(n_freq, dtype=jnp.float32) / n_freq)
    ang = jnp.stack([row[:, None] * inv_freq, col[:, None] * inv_freq], axis=1)
    return jnp.cos(ang), jnp.sin(ang)

def apply_rope(x, cos, sin):
    xf = x.astype(jnp.float32).reshape(x.shape[:-1] + (2, 2, HEAD_DIM // 4))
    x1, x2 = xf[..., 0, :], xf[..., 1, :]
    out = jnp.stack([x1 * cos - x2 * sin, x2 * cos + x1 * sin], axis=-2)
    return out.reshape(x.shape).astype(x.dtype)

def q_heads(q):
    b, n, _ = q.shape
    return q.reshape(b, n, N_KV_HEADS, Q_PER_KV, HEAD_DIM).transpose(0, 2, 3, 1, 4)

def kv_heads(k):
    b, n, _ = k.shape
    return k.reshape(b, n, N_KV_HEADS, HEAD_DIM).transpose(0, 2, 1, 3)

def gqa_blocks(q, k, v):
    b, kvh, g, n, dh = q.shape
    nb = n // Q_BLOCK
    qb = jnp.moveaxis(q.reshape(b, kvh, g, nb, Q_BLOCK, dh), 3, 0)

    def one_block(qblk):
        s = jnp.einsum('bkgqd,bkmd->bkgqm', qblk, k).astype(jnp.float32)
        p = jax.nn.softmax(s, axis=-1).astype(v.dtype)
        return jnp.einsum('bkgqm,bkmd->bkgqd', p, v)

    o = lax.map(one_block, qb)
    o = jnp.moveaxis(o, 0, 3).reshape(b, kvh, g, n, dh)
    return o.transpose(0, 3, 1, 2, 4).reshape(b, n, ATTN_DIM)

def chunk_gmlp(u, vg, w_s, b_s, g_norm):
    b, n, _ = u.shape
    u = jax.nn.gelu(u)
    vg = group_layernorm(jax.nn.gelu(vg).reshape(b, n, N_GMLP_GROUPS, GMLP_GROUP_DIM),
                         g_norm.reshape(N_GMLP_GROUPS, GMLP_GROUP_DIM))
    vc = vg.reshape(b, n // CHUNK, CHUNK, N_GMLP_GROUPS, GMLP_GROUP_DIM)
    mixed = jnp.einsum('gpq,bnqgc->bnpgc', w_s, vc) + b_s.T[None, None, :, :, None]
    return u * mixed.reshape(b, n, GMLP_DIM)

def sqrelu_mlp(h, w1, w2):
    return jnp.square(jax.nn.relu(h @ w1)) @ w2

def first_inputs(seed: int = 0) -> dict:
    key = jax.random.key(seed)
    ks = jax.random.split(key, 17)
    f32 = jnp.float32
    nrm = lambda k, shape, s: (jax.random.normal(k, shape, f32) * s)
    gain = lambda k, shape: 1.0 + 0.02 * jax.random.normal(k, shape, f32)
    return {
        "x": nrm(ks[0], (BATCH, SEQ, D_MODEL), 1.0),
        "c": nrm(ks[1], (BATCH, D_MODEL), 1.0),
        "ctx": nrm(ks[2], (BATCH, CTX_LEN, D_MODEL), 1.0),
        "c_ctx": nrm(ks[3], (D_MODEL,), 1.0),
        "w_mod": nrm(ks[4], (DEPTH, D_MODEL, N_MOD * D_MODEL), D_MODEL ** -0.5),
        "b_mod": nrm(ks[5], (DEPTH, N_MOD * D_MODEL), 0.02),
        "norm1_g": gain(ks[6], (DEPTH, D_MODEL)),
        "w_in": nrm(ks[7], (DEPTH, D_MODEL, IN_DIM), D_MODEL ** -0.5),
        "q_norm_g": gain(ks[8], (DEPTH, HEAD_DIM)),
        "k_norm_g": gain(ks[9], (DEPTH, HEAD_DIM)),
        "gmlp_norm_g": gain(ks[10], (DEPTH, GMLP_DIM)),
        "w_spatial": nrm(ks[11], (DEPTH, N_GMLP_GROUPS, CHUNK, CHUNK), CHUNK ** -0.5),
        "b_spatial": gain(ks[12], (DEPTH, N_GMLP_GROUPS, CHUNK)),
        "w_out": nrm(ks[13], (DEPTH, MIX_DIM, D_MODEL), MIX_DIM ** -0.5),
        "norm2_g": gain(ks[14], (DEPTH, D_MODEL)),
        "w_ff1": nrm(ks[15], (DEPTH, D_MODEL, FF_DIM), D_MODEL ** -0.5),
        "w_ff2": nrm(ks[16], (DEPTH, FF_DIM, D_MODEL), FF_DIM ** -0.5),
    }

def first_block(x, c, ctx, c_ctx, w_mod, b_mod, norm1_g, w_in, q_norm_g, k_norm_g, gmlp_norm_g,
              w_spatial, b_spatial, w_out, norm2_g, w_ff1, w_ff2):
    n_lat = x.shape[1]
    cos, sin = axial_rope_tables(n_lat)
    q_scale = HEAD_DIM ** -0.5
    kv_lo, kv_hi = ATTN_DIM, ATTN_DIM + 2 * KV_DIM
    x_lat, x_ctx = x, ctx
    for l in range(DEPTH):
        last = l == DEPTH - 1
        m_lat = modulation(c, w_mod[l], b_mod[l])
        m_ctx = modulation(c_ctx, w_mod[l], b_mod[l])
        sh1, sc1, ga1, sh2, sc2, ga2 = [m_lat[:, i, None, :] for i in range(N_MOD)]
        csh1, csc1, cga1, csh2, csc2, cga2 = [m_ctx[None, i, None, :] for i in range(N_MOD)]

        h_lat = modulate(rmsnorm(x_lat, norm1_g[l]), sh1, sc1)
        h_ctx = modulate(rmsnorm(x_ctx, norm1_g[l]), csh1, csc1)
        z_lat = h_lat @ w_in[l]
        q_l = z_lat[..., :ATTN_DIM]
        k_l = z_lat[..., kv_lo:kv_lo + KV_DIM]
        v_l = z_lat[..., kv_lo + KV_DIM:kv_hi]
        u_l = z_lat[..., kv_hi:kv_hi + GMLP_DIM]
        g_l = z_lat[..., kv_hi + GMLP_DIM:]
        if last:
            z_ctx = h_ctx @ w_in[l][:, kv_lo:kv_hi]
            k_c, v_c = z_ctx[..., :KV_DIM], z_ctx[..., KV_DIM:]
        else:
            z_ctx = h_ctx @ w_in[l]
            q_c = z_ctx[..., :ATTN_DIM]
            k_c = z_ctx[..., kv_lo:kv_lo + KV_DIM]
            v_c = z_ctx[..., kv_lo + KV_DIM:kv_hi]
            u_c = z_ctx[..., kv_hi:kv_hi + GMLP_DIM]
            g_c = z_ctx[..., kv_hi + GMLP_DIM:]

        qh_l = apply_rope(rmsnorm(q_heads(q_l), q_norm_g[l]), cos, sin) * q_scale
        kh_l = apply_rope(rmsnorm(kv_heads(k_l), k_norm_g[l]), cos, sin)
        kh_c = rmsnorm(kv_heads(k_c), k_norm_g[l])
        vh_c = kv_heads(v_c)
        k_all = jnp.concatenate([kh_c, kh_l], axis=2)
        v_all = jnp.concatenate([vh_c, kv_heads(v_l)], axis=2)
        attn_lat = gqa_blocks(qh_l, k_all, v_all)
        gm_lat = chunk_gmlp(u_l, g_l, w_spatial[l], b_spatial[l], gmlp_norm_g[l])
        x_lat = x_lat + ga1 * (jnp.concatenate([attn_lat, gm_lat], axis=-1) @ w_out[l])
        x_lat = x_lat + ga2 * sqrelu_mlp(modulate(rmsnorm(x_lat, norm2_g[l]), sh2, sc2),
                                         w_ff1[l], w_ff2[l])

        if not last:
            qh_c = rmsnorm(q_heads(q_c), q_norm_g[l]) * q_scale
            attn_ctx = gqa_blocks(qh_c, kh_c, vh_c)
            gm_ctx = chunk_gmlp(u_c, g_c, w_spatial[l], b_spatial[l], gmlp_norm_g[l])
            x_ctx = x_ctx + cga1 * (jnp.concatenate([attn_ctx, gm_ctx], axis=-1) @ w_out[l])
            x_ctx = x_ctx + cga2 * sqrelu_mlp(modulate(rmsnorm(x_ctx, norm2_g[l]), csh2, csc2),
                                              w_ff1[l], w_ff2[l])
    return x_lat


D_MIX = 1024
MLA_HEADS = 6
MLA_Q_RANK = 256
MLA_KV_RANK = 128
MLA_NOPE = 64
MLA_ROPE = 32
MLA_V = 64
POOL_WINDOWS = (2, 4, 8, 16)
POOL_GROUP = 64
POOL_WIDTH = POOL_GROUP * len(POOL_WINDOWS)
FOX_HEADS = 6
FOX_HEAD_DIM = 64
FOX_GATE_BIAS_INIT = 2.0
BLOCK_Q = 128
D_FF = 2816
IN_Q_A = MLA_Q_RANK
IN_KV_A = MLA_KV_RANK
IN_K_ROPE = MLA_ROPE
IN_POOL = POOL_WIDTH
IN_FOX_QKV = 3 * FOX_HEADS * FOX_HEAD_DIM
IN_FOX_F = FOX_HEADS
N_IN = IN_Q_A + IN_KV_A + IN_K_ROPE + IN_POOL + IN_FOX_QKV + IN_FOX_F


def rmsnorm_2(x, g):
    xf = x.astype(jnp.float32)
    y = xf * lax.rsqrt(jnp.mean(xf * xf, axis=-1, keepdims=True) + EPS)
    return y.astype(x.dtype) * g

def rope(x, pos):
    r = x.shape[-1]
    inv_freq = ROPE_THETA ** (-jnp.arange(0, r, 2, dtype=jnp.float32) / r)
    ang = pos.astype(jnp.float32)[:, None] * inv_freq[None, :]
    cos = jnp.cos(ang).astype(x.dtype)
    sin = jnp.sin(ang).astype(x.dtype)
    x1, x2 = x[..., : r // 2], x[..., r // 2:]
    return jnp.concatenate([x1 * cos - x2 * sin, x2 * cos + x1 * sin], axis=-1)

def causal_block_attention(q, k, v, scale, log_decay_cum=None):
    b, h, s, dk = q.shape
    dv = v.shape[-1]
    nb = s // BLOCK_Q
    qb = q.reshape(b, h, nb, BLOCK_Q, dk).transpose(2, 0, 1, 3, 4)
    kpos = jnp.arange(s)
    xs = (jnp.arange(nb), qb)
    if log_decay_cum is not None:
        xs = xs + (log_decay_cum.reshape(b, h, nb, BLOCK_Q).transpose(2, 0, 1, 3),)

    def one_block(args):
        i, q_blk = args[0], args[1]
        sc = jnp.einsum('bhqd,bhkd->bhqk', q_blk, k, preferred_element_type=jnp.float32) * scale
        if log_decay_cum is not None:
            c_blk = args[2]
            sc = sc + c_blk[..., :, None] - log_decay_cum[..., None, :].astype(jnp.float32)
        qpos = i * BLOCK_Q + jnp.arange(BLOCK_Q)
        sc = jnp.where(kpos[None, :] <= qpos[:, None], sc, -jnp.inf)
        p = jax.nn.softmax(sc, axis=-1).astype(v.dtype)
        return jnp.einsum('bhqk,bhkd->bhqd', p, v)

    out = lax.map(one_block, xs)
    return out.transpose(1, 2, 0, 3, 4).reshape(b, h, s, dv)

def mla_mixer(q_a, kv_a, k_rope, q_a_norm, w_q_b, kv_a_norm, w_kv_b, pos):
    b, s, _ = q_a.shape
    q = (rmsnorm_2(q_a, q_a_norm) @ w_q_b).reshape(b, s, MLA_HEADS, MLA_NOPE + MLA_ROPE).transpose(0, 2, 1, 3)
    q_nope, q_pe = q[..., :MLA_NOPE], rope(q[..., MLA_NOPE:], pos)
    kv = (rmsnorm_2(kv_a, kv_a_norm) @ w_kv_b).reshape(b, s, MLA_HEADS, MLA_NOPE + MLA_V).transpose(0, 2, 1, 3)
    k_nope, v = kv[..., :MLA_NOPE], kv[..., MLA_NOPE:]
    k_pe = jnp.broadcast_to(rope(k_rope, pos)[:, None], (b, MLA_HEADS, s, MLA_ROPE))
    qf = jnp.concatenate([q_nope, q_pe], axis=-1)
    kf = jnp.concatenate([k_nope, k_pe], axis=-1)
    o = causal_block_attention(qf, kf, v, 1.0 / math.sqrt(MLA_NOPE + MLA_ROPE))
    return o.transpose(0, 2, 1, 3).reshape(b, s, MLA_HEADS * MLA_V)

def pool_mixer(u, pool_w, pool_scale):
    b, s, _ = u.shape
    ng = len(POOL_WINDOWS)
    ug = u.reshape(b, s, ng, POOL_GROUP)
    cs = jnp.cumsum(ug.astype(jnp.float32), axis=1)
    count = jnp.arange(1, s + 1, dtype=jnp.float32)
    means = []
    for g, w in enumerate(POOL_WINDOWS):
        c = cs[:, :, g]
        prev = jnp.pad(c[:, : s - w], ((0, 0), (w, 0), (0, 0)))
        means.append((c - prev) / jnp.minimum(count, float(w))[None, :, None])
    pooled = jnp.stack(means, axis=2).astype(u.dtype) - ug
    y = jnp.einsum('bsgc,gcd->bsgd', pooled, pool_w)
    return y.reshape(b, s, POOL_WIDTH) * pool_scale

def fox_mixer(qkv, f_logit, fox_b_f):
    b, s, _ = qkv.shape
    qkv = qkv.reshape(b, s, 3, FOX_HEADS, FOX_HEAD_DIM).transpose(2, 0, 3, 1, 4)
    q, k, v = qkv[0], qkv[1], qkv[2]
    log_f = jax.nn.log_sigmoid((f_logit + fox_b_f).astype(jnp.float32))
    cum = jnp.cumsum(log_f, axis=1).transpose(0, 2, 1)
    o = causal_block_attention(q, k, v, 1.0 / math.sqrt(FOX_HEAD_DIM), cum)
    return o.transpose(0, 2, 1, 3).reshape(b, s, FOX_HEADS * FOX_HEAD_DIM)

def swiglu(h, w_gu, w_down):
    gu = h @ w_gu
    g, u = gu[..., :D_FF], gu[..., D_FF:]
    return (jax.nn.silu(g) * u) @ w_down

def hybrid_mixing(h, w_in, q_a_norm, w_q_b, kv_a_norm, w_kv_b, pool_w, pool_scale, fox_b_f, w_out, pos):
    z = h @ w_in
    o0 = 0
    o1 = o0 + IN_Q_A
    o2 = o1 + IN_KV_A
    o3 = o2 + IN_K_ROPE
    o4 = o3 + IN_POOL
    o5 = o4 + IN_FOX_QKV
    o6 = o5 + IN_FOX_F
    ya = mla_mixer(z[..., o0:o1], z[..., o1:o2], z[..., o2:o3], q_a_norm, w_q_b, kv_a_norm, w_kv_b, pos)
    yb = pool_mixer(z[..., o3:o4], pool_w, pool_scale)
    yc = fox_mixer(z[..., o4:o5], z[..., o5:o6], fox_b_f)
    return jnp.concatenate([ya, yb, yc], axis=-1) @ w_out

def second_inputs(seed: int = 0) -> dict:
    key = jax.random.key(seed)
    ks = jax.random.split(key, 24)
    L, D, F = DEPTH, D_MODEL, D_FF
    f32 = jnp.float32

    def nrm(k, shape, fan_in):
        return jax.random.normal(k, shape, f32) * (fan_in ** -0.5)

    def gain(k, shape):
        return 1.0 + 0.02 * jax.random.normal(k, shape, f32)

    return {
        "x": jax.random.normal(ks[0], (BATCH, SEQ, D), f32),
        "ffn1_norm": gain(ks[1], (L, D)),
        "ffn1_w_gu": nrm(ks[2], (L, D, 2 * F), D),
        "ffn1_w_down": nrm(ks[3], (L, F, D), F),
        "mix_norm": gain(ks[4], (L, D)),
        "w_in": nrm(ks[5], (L, D, N_IN), D),
        "q_a_norm": gain(ks[6], (L, MLA_Q_RANK)),
        "w_q_b": nrm(ks[7], (L, MLA_Q_RANK, MLA_HEADS * (MLA_NOPE + MLA_ROPE)), MLA_Q_RANK),
        "kv_a_norm": gain(ks[8], (L, MLA_KV_RANK)),
        "w_kv_b": nrm(ks[9], (L, MLA_KV_RANK, MLA_HEADS * (MLA_NOPE + MLA_V)), MLA_KV_RANK),
        "pool_w": nrm(ks[10], (L, len(POOL_WINDOWS), POOL_GROUP, POOL_GROUP), POOL_GROUP),
        "pool_scale": gain(ks[11], (L, POOL_WIDTH)),
        "fox_b_f": FOX_GATE_BIAS_INIT + 0.5 * jax.random.normal(ks[12], (L, FOX_HEADS), f32),
        "w_out": nrm(ks[13], (L, D_MIX, D), D_MIX),
        "ffn2_norm": gain(ks[14], (L, D)),
        "ffn2_w_gu": nrm(ks[15], (L, D, 2 * F), D),
        "ffn2_w_down": nrm(ks[16], (L, F, D), F),
        "final_norm": gain(ks[17], (D,)),
    }

def second_block(x, ffn1_norm, ffn1_w_gu, ffn1_w_down, mix_norm, w_in, q_a_norm, w_q_b, kv_a_norm, w_kv_b,
              pool_w, pool_scale, fox_b_f, w_out, ffn2_norm, ffn2_w_gu, ffn2_w_down, final_norm):
    pos = jnp.arange(x.shape[1], dtype=jnp.int32)
    for l in range(DEPTH):
        x = x + 0.5 * swiglu(rmsnorm_2(x, ffn1_norm[l]), ffn1_w_gu[l], ffn1_w_down[l])
        x = x + hybrid_mixing(rmsnorm_2(x, mix_norm[l]), w_in[l], q_a_norm[l], w_q_b[l], kv_a_norm[l], w_kv_b[l],
                              pool_w[l], pool_scale[l], fox_b_f[l], w_out[l], pos)
        x = x + 0.5 * swiglu(rmsnorm_2(x, ffn2_norm[l]), ffn2_w_gu[l], ffn2_w_down[l])
    return rmsnorm_2(x, final_norm)


def setup_inputs(seed=0):
    out = dict(first_inputs(seed))
    for name, value in second_inputs(seed + 1).items():
        if name != "x":
            out[name + "_2"] = value
    return out


def reference(
    x, c, ctx, c_ctx, w_mod, b_mod, norm1_g, w_in, q_norm_g, k_norm_g, gmlp_norm_g, w_spatial,
    b_spatial, w_out, norm2_g, w_ff1, w_ff2, ffn1_norm_2, ffn1_w_gu_2, ffn1_w_down_2,
    mix_norm_2, w_in_2, q_a_norm_2, w_q_b_2, kv_a_norm_2, w_kv_b_2, pool_w_2, pool_scale_2,
    fox_b_f_2, w_out_2, ffn2_norm_2, ffn2_w_gu_2, ffn2_w_down_2, final_norm_2,
):
    x = first_block(
        x, c, ctx, c_ctx, w_mod, b_mod, norm1_g, w_in, q_norm_g, k_norm_g, gmlp_norm_g,
        w_spatial, b_spatial, w_out, norm2_g, w_ff1, w_ff2,
    )
    return second_block(
        x, ffn1_norm_2, ffn1_w_gu_2, ffn1_w_down_2, mix_norm_2, w_in_2, q_a_norm_2, w_q_b_2,
        kv_a_norm_2, w_kv_b_2, pool_w_2, pool_scale_2, fox_b_f_2, w_out_2, ffn2_norm_2,
        ffn2_w_gu_2, ffn2_w_down_2, final_norm_2,
    )


_drawn_inputs = setup_inputs


def setup_inputs(seed=0):
    import zlib

    import numpy as np

    out = dict(_drawn_inputs(seed))
    spreads = {}
    factors = {'ctx': 3.222,
     'norm1_g': 4.04,
     'q_norm_g': 8.0,
     'k_norm_g': 8.0,
     'gmlp_norm_g': 6.942,
     'b_spatial': 7.113,
     'norm2_g': 2.79,
     'ffn1_norm_2': 8.0,
     'mix_norm_2': 7.382,
     'q_a_norm_2': 8.0,
     'kv_a_norm_2': 21.626,
     'pool_scale_2': 8.0,
     'ffn2_norm_2': 8.0,
     'final_norm_2': 7.877}
    for name, (base, spread) in spreads.items():
        noise = np.random.default_rng([zlib.crc32(name.encode()), seed]).standard_normal(out[name].shape)
        drawn = base * np.exp(spread * noise) if base else spread * noise
        out[name] = __import__('jax').numpy.asarray(drawn.astype(out[name].dtype))
    for name, factor in factors.items():
        out[name] = (out[name] * factor).astype(out[name].dtype)
    return out
```

```python
import math

import numpy as np

import concourse.bass as bass
from concourse import mybir

F32 = mybir.dt.float32
F32R = mybir.dt.float32r
ALU = mybir.AluOpType
ACT = mybir.ActivationFunctionType
AX = mybir.AxisListType

P = 128
D = 1024
KD = D // P
T = 512
C = 256
TT = T // P
CT = C // P
EPS = 1e-6
L = 2
HD = 64
Q_TILES = 4
FF1_GROUPS = 4
F2 = 2816
F2_TILES = F2 // P
F2_GROUPS = 2
FG = F2_TILES // F2_GROUPS
WMAX = FG * P
N_IN2 = 1830
MLA_D = 96
MLA_H = 6
FOX_H = 6
BANK = 512
NEG = -1e38

K_IDENT, K_AVG_D, K_AVG256, K_AVG128, K_AVG64, K_ROT64, K_ROTM, K_MASK = [i * P for i in range(8)]
K_ROPE1 = 8 * P
K_ROPE2 = K_ROPE1 + 2 * T
K_POOL = K_ROPE2 + 2 * T
K_POOLW = K_POOL + 32
K_COLS = K_POOLW + 2


def shape_constants():
    f = np.float32
    t = np.zeros((P, K_COLS), f)
    t[:, K_IDENT:K_IDENT + P] = np.eye(P, dtype=f)
    t[:, K_AVG_D:K_AVG_D + P] = 1.0 / D
    t[:, K_AVG256:K_AVG256 + P] = 1.0 / 256
    t[:, K_AVG128:K_AVG128 + P] = 1.0 / 128
    t[:, K_AVG64:K_AVG64 + P] = np.kron(np.eye(2, dtype=f), np.full((HD, HD), 1.0 / HD, f))
    rot32 = np.zeros((32, 32), f)
    for i in range(16):
        rot32[i, 16 + i] = -1.0
        rot32[16 + i, i] = 1.0
    t[:, K_ROT64:K_ROT64 + P] = np.kron(np.eye(4, dtype=f), rot32).T
    rotm = np.zeros((P, P), f)
    rotm[64:96, 64:96] = rot32
    t[:, K_ROTM:K_ROTM + P] = rotm.T
    t[:, K_MASK:K_MASK + P] = np.where(np.arange(P)[None, :] <= np.arange(P)[:, None], f(0), f(NEG))
    freq = (f(10000.0) ** (-np.arange(16, dtype=f) / f(16))).astype(f)
    pos = np.arange(T, dtype=f)
    row = np.repeat(np.arange(T // 64, dtype=f), 64)
    col = np.tile(np.arange(64, dtype=f), T // 64)
    for p in range(P):
        ang = (row if (p % HD) < 32 else col) * freq[p % 16]
        t[p, K_ROPE1:K_ROPE1 + T] = np.cos(ang)
        t[p, K_ROPE1 + T:K_ROPE1 + 2 * T] = np.sin(ang)
    freq2 = (f(10000.0) ** (-np.arange(0, 32, 2, dtype=f) / f(32))).astype(f)
    t[:, K_ROPE2:K_ROPE2 + T] = 1.0
    for p in range(64, 96):
        ang = pos * freq2[p % 16]
        t[p, K_ROPE2:K_ROPE2 + T] = np.cos(ang)
        t[p, K_ROPE2 + T:K_ROPE2 + 2 * T] = np.sin(ang)
    for j in range(2):
        for half in range(2):
            w = 2 ** (2 * j + half + 1)
            rows = slice(64 * half, 64 * half + 64)
            t[rows, K_POOL + 16 * j:K_POOL + 16 * j + 16] = 1.0 / np.minimum(np.arange(1, 17), w).astype(f)
            t[rows, K_POOLW + j] = 1.0 / w
    return t


R_N1, R_N2, R_GM, R_F1, R_MX, R_F2, R_FIN, R_QA, R_KVA, R_PS, R_C, R_QK, R_FB = (
    0, 16, 32, 40, 56, 72, 88, 96, 100, 102, 106, 122, 126)


def build_program(nc, a, out):
    from contextlib import ExitStack
    ctx = ExitStack()
    with ctx:
        slab = ctx.enter_context(nc.sbuf_tensor("slab", [P, 53120], F32))
        at = [nc.sbuf_base - 53120 * 4]

        def place(name, shape, dt=F32, offset=None):
            size = 4 * int(np.prod(shape[1:]))
            where = at[0] if offset is None else offset
            t = nc.alloc_sbuf_tensor_at(name, shape, dt, offset=where)
            if offset is None:
                at[0] += -(-size // 32) * 32
                assert at[0] <= base0 + 53120 * 4, name
            return t

        base0 = at[0]
        x_lat = place("x_lat", [P, KD, T])
        x_ctx = place("x_ctx", [P, KD, C])
        hh_lat = place("hh_lat", [P, KD, T], F32R)
        hl_lat = place("hl_lat", [P, KD, T], F32R)
        hh_ctx = place("hh_ctx", [P, KD, C], F32R)
        hl_ctx = place("hl_ctx", [P, KD, C], F32R)
        mid0 = at[0]
        m1h_lat = place("m1h_lat", [P, 8, T], F32R)
        m1l_lat = place("m1l_lat", [P, 8, T], F32R)
        m1h_ctx = place("m1h_ctx", [P, 8, C], F32R)
        m1l_ctx = place("m1l_ctx", [P, 8, C], F32R)
        m2h = place("m2h", [P, FG, T], F32R, mid0)
        m2l = place("m2l", [P, FG, T], F32R, mid0 + FG * T * 4)
        scr = place("scr", [P, 12288], F32, mid0)
        z = place("z", [P, 14 * (T + C)])
        w_raw = place("w_raw", [P, 2, WMAX])
        w_hi_sb = place("w_hi_sb", [P, 2, WMAX], F32R)
        w_lo_sb = place("w_lo_sb", [P, 2, WMAX], F32R)
        konst = place("konst", [P, 8 * P])
        rope = place("rope", [P, 2, T])
        pool_k = place("pool_k", [P, 34])
        pc = place("pc", [P, P])
        bmod = place("bmod", [P, 96])
        modv = place("modv", [P, L, 48, 2])
        gains = place("gains", [P, L, 2, 2, KD])
        silu_c = place("silu_c", [P, 2, KD])
        stats = place("stats", [P, 4, 6])
        mv = place("mv", [P, 4, 2])
        grs = place("grs", [P, 4, 1])
        nmax = place("nmax", [P, 2])
        rsum = place("rsum", [P, 2])
        rinv = place("rinv", [P, 2])
        zero_col = place("zero_col", [P, 1])
        eps_col = place("eps_col", [P, 1])
        ps = ctx.enter_context(nc.psum_tensor("ps", [P, 8 * BANK], F32))

        ident = konst[:, K_IDENT:K_IDENT + P]

        def bank(b, n=BANK):
            return ps[:, b * BANK:b * BANK + n]

        def zt(i, s="lat"):
            if s == "lat":
                return z[:, i * T:(i + 1) * T]
            return z[:, 14 * T + i * C:14 * T + (i + 1) * C]

        X = {"lat": x_lat, "ctx": x_ctx}
        HH = {"lat": hh_lat, "ctx": hh_ctx}
        HL = {"lat": hl_lat, "ctx": hl_ctx}
        W = {"lat": T, "ctx": C}

        names = ("w_hi w_lo chunk_done z_taken silu_taken relu_ready t_ready mid_hi mid_lo r_taken "
                 "sq_done sumsq sum_ready root_ready rstd_ready norm_t h_hi h_lo "
                 "mod_used mod_taken ws_turned ws_copied g_turned g_var g_root g_hat g_mixed gm_t gm_hi gm_lo "
                 "q_sq q_ms q_root q_rs q_n q_rot q_fin k_dup v_turned v_copied "
                 "s_ready s_max p_exp p_norm p_turned pt_act pt_dve pv_done ao_copied ao_hi ao_lo "
                 "mla_sq mla_ms mla_root mla_n mla_q mla_qc mla_rot mla_qf mla_k mla_kc mla_v mla_vc "
                 "fox_q fox_vt fox_vc fox_a fox_e fox_c bd_zero pool_m pool_y pool_t pool_hi pool_lo "
                 "rows_zero rows_turned rows_copied silu_done x_turned x_copied y_ready y_turned y_copied "
                 "dve_chain act_chain pool_chain").split()
        dma_names = ("w_loaded0 w_loaded1 mod_loaded0 mod_loaded1 mod_loaded2 mod_loaded3 konst_loaded rows_loaded "
                     "x_loaded rope_loaded ws_loaded mla_loaded bd_loaded stored").split()
        S = {n: ctx.enter_context(nc.semaphore(n)) for n in names + dma_names}
        w_loaded = [S["w_loaded0"], S["w_loaded1"]]
        mod_loaded = [S[f"mod_loaded{i}"] for i in range(4)]

        stages = []
        totals = {n: 0 for n in names + dma_names}
        for n in ("z_taken", "r_taken", "t_ready", "relu_ready", "mid_lo"):
            totals[n] = 2
        totals["silu_taken"] = 1

        class Stage:
            def __init__(self, kind, counts, chunks=0, **spec):
                self.kind, self.spec = kind, spec
                self.chunk0 = sum(s.chunks for s in stages)
                self.chunks = chunks
                self.base = dict(totals)
                for n, k in counts.items():
                    totals[n] += k
                stages.append(self)

            def __getattr__(self, n):
                return self.spec[n]

            def at(self, name, k):
                return self.base[name] + k

        def add_norm(sets, a_col, b_col, to_h=True, own_sum=False):
            Stage("norm", dict(sum_ready=1, root_ready=1, rstd_ready=1, norm_t=KD * len(sets), h_hi=KD * len(sets),
                               h_lo=KD * len(sets)), sets=sets, a_col=a_col, b_col=b_col, to_h=to_h)

        def col(r):
            return lambda s, m: pc[:, r + m:r + m + 1]

        def no_shift(s, m):
            return zero_col[:, 0:1]

        Stage("setup", dict(sumsq=1))
        Stage("mod", dict(mod_used=2 * 24, mod_taken=2 * 12), l=0)
        for l in range(L):
            both = ("lat", "ctx")
            more = both if l < L - 1 else ("lat",)

            def a_col(i, l=l):
                return lambda s, m: gains[:, l, i, 0 if s == "lat" else 1, m:m + 1]

            def b_col(i, l=l):
                return lambda s, m: modv[:, l, 24 * i + m, (0 if s == "lat" else 1):(1 if s == "lat" else 2)]

            def gate(i, l=l):
                return lambda s, m: modv[:, l, bass.ds(24 * i + 16 + m, 1), 0 if s == "lat" else 1]

            add_norm(both, a_col(0), b_col(0))
            Stage("linear_z", dict(z_taken=14), 14, w="w_in", l=l, sets=both, more=more)
            Stage("spatial", dict(ws_turned=1, ws_copied=1, g_turned=TT + CT * (len(more) - 1), g_mixed=len(more),
                                  g_hat=TT + CT * (len(more) - 1), g_var=TT + CT * (len(more) - 1),
                                  g_root=TT + CT * (len(more) - 1), gm_t=4 * len(more), gm_hi=4 * len(more),
                                  gm_lo=4 * len(more), ws_loaded=80), l=l, sets=more)
            nqk = 5 + (5 if l < L - 1 else 1)
            Stage("qk_heads", dict(q_sq=nqk, q_ms=nqk, q_root=nqk, q_rs=nqk, q_n=nqk, q_rot=5, q_fin=5, k_dup=1, v_turned=1,
                                   v_copied=1), l=l, sets=more)
            for s in more[::-1]:
                nq = W[s] // P
                keys = C + T if s == "lat" else C
                U = 8 * nq
                groups = U * (2 if keys > BANK else 1)
                Stage("attention", dict(s_ready=U, s_max=U, p_exp=U, p_norm=U, p_turned=groups,
                                        pt_act=groups // 2, pt_dve=groups - groups // 2, pv_done=8, ao_copied=8,
                                        ao_hi=4, ao_lo=4), first=True, s=s, l=l, nq=nq, heads=8)
            Stage("linear_r", dict(r_taken=8, sq_done=8, sumsq=1), 8, src="w_out", l=l, sets=more, gate=gate(0), group=None,
                  final=True, kt=KD)
            add_norm(more, a_col(1), b_col(1))
            for g in range(FF1_GROUPS):
                Stage("linear_sqrelu", dict(relu_ready=8, t_ready=8, mid_hi=8, mid_lo=8), 8, l=l, sets=more, group=g)
                last = g == FF1_GROUPS - 1
                Stage("linear_r", dict(r_taken=8, sq_done=8 * last, sumsq=1 * last), 8, src="w_ff2", l=l, sets=more,
                      gate=gate(1), group=g, final=last, kt=KD)
        lat = ("lat",)
        for l in range(L):
            def half(s, m):
                return 0.5

            def one(s, m):
                return 1.0

            for part in ("ffn1", "mix", "ffn2"):
                if part == "mix":
                    add_norm(lat, col(R_MX + KD * l), no_shift)
                    Stage("linear_z2", dict(z_taken=16), 16, l=l, sets=lat)
                    Stage("mixer2", dict(bd_zero=1, pool_m=2, pool_y=2, pool_t=2, pool_hi=2, pool_lo=2, fox_q=3, fox_vt=3,
                                         fox_vc=3, fox_a=1, fox_e=2, fox_c=1, mla_sq=3, mla_ms=2, mla_root=2, mla_n=3, mla_q=6,
                                         mla_qc=6, mla_rot=7, mla_qf=7, mla_k=6, mla_kc=12, mla_v=4, mla_vc=4,
                                         mla_loaded=32, bd_loaded=64), l=l)
                    U = 12 * TT
                    Stage("attention", dict(s_ready=U, s_max=U, p_exp=U, p_norm=U, p_turned=U, pt_act=U // 2,
                                            pt_dve=U - U // 2, pv_done=12, ao_copied=12, ao_hi=6, ao_lo=6),
                          first=False, s="lat", l=l, nq=TT, heads=12)
                    Stage("linear_r", dict(r_taken=8, sq_done=8, sumsq=1), 8, src="w_out_2", l=l, sets=lat, gate=one,
                          group=None, final=True, kt=KD)
                else:
                    add_norm(lat, col((R_F1 if part == "ffn1" else R_F2) + KD * l), no_shift)
                    for g in range(F2_GROUPS):
                        Stage("linear_glu", dict(silu_taken=FG, t_ready=FG, mid_hi=FG, mid_lo=FG), 2 * FG, l=l, sets=lat,
                              group=g, part=part)
                        last = g == F2_GROUPS - 1
                        Stage("linear_r", dict(r_taken=8, sq_done=8 * last, sumsq=1 * last), 8,
                              src=part + "_w_down_2", l=l, sets=lat, gate=half, group=g, final=last, kt=FG)
        add_norm(lat, col(R_FIN), no_shift, to_h=False)
        Stage("store", dict(y_turned=TT, y_copied=2 * TT))
        linear = [s for s in stages if s.chunks]
        n_chunks = sum(s.chunks for s in stages)

        def kt_of(st):
            return st.spec.get("kt", KD)

        def next_kt(st):
            i = linear.index(st)
            return kt_of(linear[i + 1]) if i + 1 < len(linear) else None

        def chunk_pairs(eng, st, body):
            n = st.chunks // 2
            if n > 1:
                with eng.Fori(0, n - 1) as i:
                    body(i * 2, kt_of(st))
            body(st.chunks - 2, next_kt(st))

        def tile_ds(i):
            return bass.ds(i, 1)

        def mod_slot(n):
            return scr[:, n * 2048:(n + 1) * 2048].rearrange("p (k m) -> p k m", k=KD)

        ws_raw = scr[:, 0:512].rearrange("p (g q) -> p g q", g=4)
        ws_t = scr[:, 512:1024].rearrange("p (g q) -> p g q", g=4)
        ws_bias = scr[:, 1024:1536].rearrange("p (g q) -> p g q", g=4)
        gm_tmp = [scr[:, 1536 + 512 * i:2048 + 512 * i] for i in range(2)]
        qk_sq = [scr[:, 2560 + 512 * i:3072 + 512 * i] for i in range(2)]
        qk_rs = [scr[:, 3584 + 512 * i:4096 + 512 * i] for i in range(2)]
        qk_tb = scr[:, 4608:5120]
        k_all = scr[:, 5120:5888]
        k_swap = scr[:, 5888:6656]
        v_all = scr[:, 6656:7424].rearrange("p (t f) -> p t f", t=6)
        wq_b = scr[:, 0:1152].rearrange("p (k m) -> p k m", k=2)
        wkv_b = scr[:, 1152:1920]
        mla_kt = [scr[:, 1920 + 512 * i:2432 + 512 * i] for i in range(6)]
        mla_qt = [scr[:, 4992 + 512 * i:5504 + 512 * i] for i in range(6)]
        mla_sq = [scr[:, 8064 + 512 * i:8576 + 512 * i] for i in range(3)]
        mla_rs = [scr[:, 9600 + 512 * i:10112 + 512 * i] for i in range(2)]
        mla_tb = scr[:, 10624:11136]
        pool_bd = scr[:, 11136:11392].rearrange("p (j m) -> p j m", j=2)
        pool_a = scr[:, 1920:2944].rearrange("p (j t) -> p j t", j=2)
        pool_b = scr[:, 2944:3968].rearrange("p (j t) -> p j t", j=2)
        pool_tmp = scr[:, 3968:4480]
        fox_t = [scr[0:FOX_H, 4992 + 512 * i:5504 + 512 * i] for i in range(4)]
        v_mla = z[:, 16 * T:16 * T + 4 * 384].rearrange("p (t f) -> p t f", t=4)

        def att_p(st, i, n):
            p0 = 7424 if st.first else 8064
            w = 768 if st.first else 512
            return scr[:, p0 + w * i:p0 + w * i + n]

        def att_pt(st, kt, c0, c1):
            p0 = 8960 if st.first else 9088
            return scr[:, p0 + 512 * kt + c0:p0 + 512 * kt + c1]

        def att_out(st, n):
            p0 = 0 if st.first else 11136
            return scr[:, p0:p0 + n]

        norm_rs = {"lat": scr[:, 0:512], "ctx": scr[:, 512:768]}
        norm_tmp = [scr[:, 768 + 512 * i:1280 + 512 * i] for i in range(2)]
        sq_tmp = {"lat": z[:, 0:512], "ctx": z[:, 512:768]}
        sq_sum = {"lat": z[:, 768:1280], "ctx": z[:, 1280:1536]}
        ff_t = {"lat": [z[:, 2048:2560], z[:, 2560:3072]], "ctx": [z[:, 3072:3328], z[:, 3328:3584]]}
        ff_silu = z[:, 3584:4096]
        ff_r = {"lat": [z[:, 3584:4096], z[:, 4096:4608]], "ctx": [z[:, 4608:4864], z[:, 4864:5120]]}

        def n_keys(st, qt):
            if st.first:
                return C + T if st.s == "lat" else C
            return (qt + 1) * P

        def key_groups(st, qt):
            n = n_keys(st, qt) // P
            return [range(0, min(4, n))] + ([range(4, n)] if n > 4 else [])

        def unit(st, u):
            return u // st.nq, u % st.nq

        def all_groups(st):
            found = []
            for u in range(st.heads * st.nq):
                for kts in key_groups(st, unit(st, u)[1]):
                    found.append((u, kts))
            return found

        def on_act(i):
            return i % 2 == 1

        def qk_items(st):
            items = [("lat", 4), ("ctx", 4)] + [("lat", i) for i in range(4)]
            if "ctx" in st.sets:
                items += [("ctx", i) for i in range(4)]
            return items

        def k_part(s):
            return k_all[:, C:C + T] if s == "lat" else k_all[:, 0:C]

        pool_tmps = [scr[:, 3968:4480], scr[:, 4480:4992]]

        def pt_dst(st, kts, qt):
            p0 = 8960 if st.first else 9088
            if st.first and st.s == "lat":
                p0 = 8960
            n = len(kts)
            v = scr[:, p0 + 512 * kts[0]:p0 + 512 * (kts[0] + n)].rearrange("p (k q) -> p k q", q=512)
            return v[:, :, qt * P:(qt + 1) * P]

        def pt_src(i, kts):
            return bank(4 + i % 2, len(kts) * P).rearrange("p (k q) -> p k q", q=P)

        def out_tile(st, hd):
            if st.first:
                return hd // 2
            return hd // 2 if hd < MLA_H else 5 + (hd - MLA_H) // 2

        with nc.Block() as block:

            @block.sync
            def _(sp):
                def load_chunk(st, c, slot, kt, src):
                    g = c + st.chunk0
                    sp.wait_ge(S["w_lo"], g - 1)
                    width = src.shape[-1]
                    off = 64 if width == 32 else 0
                    dst = w_raw[:, slot, 0:kt * P].rearrange("p (k m) -> p k m", m=P)[:, :, off:off + width]
                    sp.dma_start(dst, src).then_inc(w_loaded[slot], 16)

                def rows_of(w, k0, kt):
                    return w[k0 * P:(k0 + kt) * P, :].rearrange("(k p) m -> p k m", p=P)

                def stream(st, kt, src_of):
                    with sp.Fori(1 if st.chunk0 == 0 else 0, st.chunks // 2) as i:
                        for slot in range(2):
                            load_chunk(st, i * 2 + slot, slot, kt, src_of(i * 2 + slot))

                for st in stages:
                    if st.kind == "setup":
                        sp.dma_start(konst[:], a["consts"][:, 0:8 * P]).then_inc(S["konst_loaded"], 16)
                        sp.dma_start(pool_k[:], a["consts"][:, K_POOL:K_POOL + 34]).then_inc(S["konst_loaded"], 16)
                        for t in range(TT):
                            sp.dma_start(z[:, t * D:(t + 1) * D], a["x"][0, t * P:(t + 1) * P, :]).then_inc(S["x_loaded"], 16)
                        for t in range(CT):
                            sp.dma_start(z[:, (TT + t) * D:(TT + t + 1) * D], a["ctx"][0, t * P:(t + 1) * P, :]
                                         ).then_inc(S["x_loaded"], 16)
                        rows = z[:, 6 * D:6 * D + P]
                        sp.wait_ge(S["rows_zero"], 1)

                        def put(r, ap, n, w=P, at_col=0):
                            sp.dma_start(rows[r:r + n, at_col:at_col + w], ap).then_inc(S["rows_loaded"], 16)

                        k8 = "l (k p) -> (l k) p"
                        put(R_N1, a["norm1_g"].rearrange(k8, p=P), 16)
                        put(R_N2, a["norm2_g"].rearrange(k8, p=P), 16)
                        put(R_GM, a["gmlp_norm_g"].rearrange(k8, p=P), 8)
                        put(R_F1, a["ffn1_norm_2"].rearrange(k8, p=P), 16)
                        put(R_MX, a["mix_norm_2"].rearrange(k8, p=P), 16)
                        put(R_F2, a["ffn2_norm_2"].rearrange(k8, p=P), 16)
                        put(R_FIN, a["final_norm_2"].rearrange("(k p) -> k p", p=P), 8)
                        put(R_QA, a["q_a_norm_2"].rearrange(k8, p=P), 4)
                        put(R_KVA, a["kv_a_norm_2"].rearrange(k8, p=P), 2)
                        put(R_PS, a["pool_scale_2"].rearrange(k8, p=P), 4)
                        put(R_C, a["c"].rearrange(k8, p=P), 8)
                        put(R_C + 8, a["c_ctx"].rearrange("(k p) -> k p", p=P), 8)
                        for half in range(2):
                            put(R_QK, a["q_norm_g"][:, :], 2, HD, HD * half)
                            put(R_QK + 2, a["k_norm_g"][:, :], 2, HD, HD * half)
                        put(R_FB, a["fox_b_f_2"][:, :], 2, FOX_H)
                        sp.dma_start(z[0:96, 6 * D + P:6 * D + 2 * P], a["b_mod"].rearrange(k8, p=P)
                                     ).then_inc(S["rows_loaded"], 16)
                        for slot in range(2):
                            sp.dma_start(w_raw[:, slot, 0:KD * P].rearrange("p (k m) -> p k m", m=P),
                                         rows_of(a["w_in"][0], 0, KD)[:, :, slot * P:(slot + 1) * P]
                                         ).then_inc(w_loaded[slot], 16)
                    elif st.kind == "mod":
                        for l in range(L):
                            src = a["w_mod"][l].rearrange("(k p) m -> p k m", p=P)
                            if l == 0:
                                for n in range(4):
                                    sp.dma_start(mod_slot(n), src[:, :, n * 256:(n + 1) * 256]).then_inc(mod_loaded[n], 16)
                            with sp.Fori(1 - l, 6) as i:
                                for n in range(4):
                                    sp.wait_ge(S["mod_used"], i * 4 + (l * 24 + n - 3))
                                    sp.dma_start(mod_slot(n), src[:, :, bass.ds(i * 1024 + n * 256, 256)]
                                                 ).then_inc(mod_loaded[n], 16)
                    elif st.kind == "linear_z":
                        if st.l == 0:
                            sp.dma_start(rope[:], a["consts"][:, K_ROPE1:K_ROPE1 + 2 * T].rearrange("p (a t) -> p a t", a=2)
                                         ).then_inc(S["rope_loaded"], 16)
                        w = rows_of(a["w_in"][st.l], 0, KD)
                        stream(st, KD, lambda c: w[:, :, bass.ds(c * P, P)])
                    elif st.kind == "linear_z2":
                        if st.l == 0:
                            sp.dma_start(rope[:], a["consts"][:, K_ROPE2:K_ROPE2 + 2 * T].rearrange("p (a t) -> p a t", a=2)
                                         ).then_inc(S["rope_loaded"], 16)
                        w = rows_of(a["w_in_2"][st.l], 0, KD)
                        for c, c0 in enumerate((0, 128, 256, 416)):
                            load_chunk(st, c, c % 2, KD, w[:, :, c0:c0 + P])
                        with sp.Fori(2, 7) as i:
                            for slot in range(2):
                                load_chunk(st, i * 2 + slot, slot, KD, w[:, :, bass.ds(i * 256 + (slot * P + 416 - 3 * P), P)])
                        load_chunk(st, 14, 0, KD, w[:, :, 384:416])
                        load_chunk(st, 15, 1, KD, w[:, :, 1824:1830])
                    elif st.kind == "linear_r":
                        w = a[st.src][st.l]
                        k0 = 0 if st.group is None else st.group * st.kt
                        w = rows_of(w, k0, st.kt)
                        stream(st, st.kt, lambda c: w[:, :, bass.ds(c * P, P)])
                    elif st.kind == "linear_sqrelu":
                        w = rows_of(a["w_ff1"][st.l], 0, KD)
                        stream(st, KD, lambda c: w[:, :, bass.ds((c + 8 * st.group) * P, P)])
                    elif st.kind == "linear_glu":
                        w = rows_of(a[st.part + "_w_gu_2"][st.l], 0, KD)
                        with sp.Fori(0, FG) as i:
                            for slot in range(2):
                                load_chunk(st, i * 2 + slot, slot, KD,
                                           w[:, :, bass.ds(i * P + (slot * F2 + st.group * FG * P), P)])
                    elif st.kind == "spatial":
                        sp.wait_ge(S["chunk_done"], st.chunk0 - 1)
                        sp.dma_start(ws_raw[:, :, :], a["w_spatial"][st.l].rearrange("g p q -> p g q")
                                     ).then_inc(S["ws_loaded"], 16)
                        for g in range(4):
                            sp.dma_start(ws_bias[:, g, :], a["b_spatial"][st.l, g:g + 1, :].to_broadcast([P, P])
                                         ).then_inc(S["ws_loaded"], 16)
                    elif st.kind == "mixer2":
                        sp.wait_ge(S["chunk_done"], st.chunk0 - 1)
                        sp.dma_start(wq_b[:, :, :], a["w_q_b_2"][st.l].rearrange("(k p) m -> p k m", p=P)
                                     ).then_inc(S["mla_loaded"], 16)
                        sp.dma_start(wkv_b[:, :], a["w_kv_b_2"][st.l]).then_inc(S["mla_loaded"], 16)
                        sp.wait_ge(S["bd_zero"], st.at("bd_zero", 1))
                        for g in range(4):
                            r = 64 * (g % 2)
                            sp.dma_start(pool_bd[r:r + 64, g // 2, r:r + 64], a["pool_w_2"][st.l, g]
                                         ).then_inc(S["bd_loaded"], 16)
                    elif st.kind == "store":
                        for t in range(TT):
                            sp.wait_ge(S["y_copied"], st.at("y_copied", 2 * (t + 1)))
                            sp.dma_start(out[0, t * P:(t + 1) * P, :], z[:, 4096 + t * D:4096 + (t + 1) * D]
                                         ).then_inc(S["stored"], 16)
                        sp.wait_ge(S["stored"], 16 * TT)

            @block.tensor
            def _(pe):
                def products(dst, wslot, kt, hi, lo, n):
                    for k in range(kt):
                        wh = w_hi_sb[:, wslot, k * P:(k + 1) * P]
                        wl = w_lo_sb[:, wslot, k * P:(k + 1) * P]
                        nc.tensor.matmul(dst, wl, hi[:, k, 0:n], start=(k == 0), stop=False)
                        nc.tensor.matmul(dst, wh, lo[:, k, 0:n], start=False, stop=False)
                        mm = nc.tensor.matmul(dst, wh, hi[:, k, 0:n], start=False, stop=(k == kt - 1))
                    return mm

                def linear_chunks(st, free, banks, xs, sets_of):
                    def pair(c, _):
                        for s in range(2):
                            g = c + (st.chunk0 + s)
                            pe.wait_ge(S["w_lo"], g + 1)
                            free(c, s)
                            for name in sets_of(c):
                                hi, lo = xs[name]
                                mm = products(bank(banks[name] + s, W[name]), s, kt_of(st), hi, lo, W[name])
                            mm.then_inc(S["chunk_done"], 1)
                    return pair

                def run_linear(st, free, banks, xs, splits=None):
                    if splits is None:
                        chunk_pairs(pe, st, linear_chunks(st, free, banks, xs, lambda c: st.sets))
                    else:
                        for first, last, sets in splits:
                            body = linear_chunks(st, free, banks, xs, lambda c: sets)
                            if last - first > 2:
                                with pe.Fori(first // 2, last // 2) as i:
                                    body(i * 2, None)
                            else:
                                body(first, None)

                h = {s: (HH[s], HL[s]) for s in W}
                mid1 = {"lat": (m1h_lat, m1l_lat), "ctx": (m1h_ctx, m1l_ctx)}
                mid2 = {"lat": (m2h, m2l)}
                up_banks = {"lat": 0, "ctx": 4}
                down_banks = {"lat": 2, "ctx": 6}

                for st in stages:
                    if st.kind == "setup":
                        pe.wait_ge(S["konst_loaded"], 32)
                        pe.wait_ge(S["x_loaded"], 16 * (TT + CT))
                        for i in range(2 * (TT + CT)):
                            if i >= 4:
                                pe.wait_ge(S["x_copied"], i - 3)
                            for j in range(4):
                                k = 4 * (i % 2) + j
                                mm = nc.tensor.transpose(bank(i % 4)[:, j * P:(j + 1) * P],
                                                         z[:, (i // 2) * D + k * P:(i // 2) * D + (k + 1) * P], ident)
                            mm.then_inc(S["x_turned"], 1)
                        pe.wait_ge(S["rows_loaded"], 16 * 18)
                        nc.tensor.transpose(bank(4, P), z[:, 6 * D:6 * D + P], ident)
                        nc.tensor.transpose(bank(5, 96), z[0:96, 6 * D + P:6 * D + 2 * P], konst[0:96, 0:96]
                                            ).then_inc(S["rows_turned"], 1)
                    elif st.kind == "mod":
                        pe.wait_ge(S["silu_done"], 1)
                        for l in range(L):
                            def blocks(i, first):
                                for n in range(4):
                                    pe.wait_ge(mod_loaded[n], i * 16 + (96 * l + 16))
                                    if n % 2 == 0 and not first:
                                        pe.wait_ge(S["mod_taken"], i * 2 + (12 * l + n // 2 - 1))
                                    for b in range(2):
                                        for k in range(KD):
                                            mm = nc.tensor.matmul(
                                                bank(6 + n // 2)[:, 4 * (n % 2) + 2 * b:4 * (n % 2) + 2 * b + 2],
                                                mod_slot(n)[:, k, b * P:(b + 1) * P], silu_c[:, :, k],
                                                start=(k == 0), stop=(k == KD - 1))
                                    mm.then_inc(S["mod_used"], 1)
                            if l == 0:
                                blocks(0, True)
                            with pe.Fori(1 - l, 6) as i:
                                blocks(i, False)
                    elif st.kind == "norm":
                        pe.wait_ge(S["sumsq"], st.at("sumsq", 0))
                        for s in st.sets:
                            mm = nc.tensor.matmul(bank(up_banks[s], W[s]), konst[:, K_AVG_D:K_AVG_D + P], sq_sum[s],
                                                  start=True, stop=True)
                        mm.then_inc(S["sum_ready"], 1)
                    elif st.kind == "linear_z":
                        pe.wait_ge(S["h_lo"], st.at("h_lo", 0))

                        def free(c, s):
                            pe.wait_ge(S["z_taken"], c + (st.at("z_taken", 0) + s - 1))
                        if st.sets == st.more:
                            run_linear(st, free, up_banks, h)
                        else:
                            run_linear(st, free, up_banks, h, [(0, 4, ("lat",)), (4, 6, st.sets), (6, 14, ("lat",))])
                    elif st.kind == "linear_z2":
                        pe.wait_ge(S["h_lo"], st.at("h_lo", 0))
                        run_linear(st, lambda c, s: pe.wait_ge(S["z_taken"], c + (st.at("z_taken", 0) + s - 1)), up_banks, h)
                    elif st.kind == "linear_sqrelu":
                        pe.wait_ge(S["h_lo"], st.at("h_lo", 0))
                        run_linear(st, lambda c, s: pe.wait_ge(S["relu_ready"], c + (st.at("relu_ready", 0) + s - 1)), up_banks, h)
                    elif st.kind == "linear_glu":
                        pe.wait_ge(S["h_lo"], st.at("h_lo", 0))

                        def free(c, s):
                            half = c // 2 if isinstance(c, int) else pair_of(c)
                            if s == 0:
                                pe.wait_ge(S["silu_taken"], half + st.at("silu_taken", 0))
                            else:
                                pe.wait_ge(S["t_ready"], half + st.at("t_ready", 0))
                        body = linear_chunks(st, free, up_banks, h, lambda c: st.sets)
                        with pe.Fori(0, FG) as i:
                            pair_of = lambda c: i
                            body(i * 2, None)
                    elif st.kind == "linear_r":
                        if st.group is None:
                            pe.wait_ge(S["ao_lo"], st.at("ao_lo", 0))
                            if "w_out" == st.src:
                                pe.wait_ge(S["gm_lo"], st.at("gm_lo", 0))
                            else:
                                pe.wait_ge(S["pool_lo"], st.at("pool_lo", 0))
                            xs = h
                        else:
                            pe.wait_ge(S["mid_lo"], st.at("mid_lo", 0))
                            xs = mid1 if st.src == "w_ff2" else mid2
                        run_linear(st, lambda c, s: pe.wait_ge(S["r_taken"], c + (st.at("r_taken", 0) + s - 1)), down_banks, xs)
                    elif st.kind == "spatial":
                        pe.wait_ge(S["ws_loaded"], st.at("ws_loaded", 80))
                        pe.wait_ge(S["z_taken"], st.at("z_taken", 0))
                        for g in range(4):
                            mm = nc.tensor.transpose(bank(6)[:, g * P:(g + 1) * P], ws_raw[:, g, :], ident)
                        mm.then_inc(S["ws_turned"], 1)
                        tiles = [(s, t) for s in st.sets for t in range(W[s] // P)]

                        def turn(i):
                            s, t = tiles[i]
                            if i >= 2:
                                pe.wait_ge(S["g_hat"], st.at("g_hat", i - 1))
                            for g in range(4):
                                mm = nc.tensor.transpose(bank(i % 2)[:, g * P:(g + 1) * P],
                                                         zt(10 + g, s)[:, t * P:(t + 1) * P], ident)
                            mm.then_inc(S["g_turned"], 1)
                        turn(0)
                        pe.wait_ge(S["ws_copied"], st.at("ws_copied", 1))
                        for i, (s, t) in enumerate(tiles):
                            if i + 1 < len(tiles):
                                turn(i + 1)
                            pe.wait_ge(S["g_hat"], st.at("g_hat", i + 1))
                            if i == TT:
                                pe.wait_ge(S["gm_t"], st.at("gm_t", 4))
                            for g in range(4):
                                mm = nc.tensor.matmul(bank(2 + g)[:, t * P:(t + 1) * P], zt(10 + g, s)[:, t * P:(t + 1) * P],
                                                      ws_t[:, g, :], start=True, stop=True)
                            if t == W[s] // P - 1:
                                mm.then_inc(S["g_mixed"], 1)
                    elif st.kind == "qk_heads":
                        pe.wait_ge(S["gm_t"], st.at("gm_t", 0))
                        pe.wait_ge(S["g_hat"], st.at("g_hat", 0))
                        for t in range(TT):
                            nc.tensor.transpose(bank(4)[:, t * P:(t + 1) * P], zt(5)[:, t * P:(t + 1) * P], ident)
                        for t in range(CT):
                            mm = nc.tensor.transpose(bank(5)[:, t * P:(t + 1) * P], zt(5, "ctx")[:, t * P:(t + 1) * P], ident)
                        mm.then_inc(S["v_turned"], 1)
                        items = qk_items(st)

                        def rot(i):
                            s, tile = items[i]
                            if s == "lat":
                                n = sum(x == "lat" for x, _ in items[:i])
                                pe.wait_ge(S["q_n"], st.at("q_n", i + 1))
                                if n >= 2:
                                    pe.wait_ge(S["q_fin"], st.at("q_fin", n - 1))
                                nc.tensor.matmul(bank(2 + n % 2), konst[:, K_ROT64:K_ROT64 + P], zt(tile),
                                                 start=True, stop=True).then_inc(S["q_rot"], 1)
                        for i, (s, tile) in enumerate(items):
                            pe.wait_ge(S["q_sq"], st.at("q_sq", i + 1))
                            if i >= 2:
                                pe.wait_ge(S["q_rs"], st.at("q_rs", i - 1))
                            nc.tensor.matmul(bank(i % 2, W[s]), konst[:, K_AVG64:K_AVG64 + P], qk_sq[i % 2][:, 0:W[s]],
                                             start=True, stop=True).then_inc(S["q_ms"], 1)
                            if i >= 1:
                                rot(i - 1)
                        rot(len(items) - 1)
                    elif st.kind == "attention":
                        if st.first:
                            pe.wait_ge(S["q_fin"], st.at("q_fin", 0))
                            pe.wait_ge(S["q_n"], st.at("q_n", 0))
                            pe.wait_ge(S["k_dup"], st.at("k_dup", 0))
                            pe.wait_ge(S["v_copied"], st.at("v_copied", 0))
                        else:
                            pe.wait_ge(S["mla_qf"], st.at("mla_qf", 0))
                            pe.wait_ge(S["mla_kc"], st.at("mla_kc", 0))
                            pe.wait_ge(S["mla_vc"], st.at("mla_vc", 0))
                            pe.wait_ge(S["fox_vc"], st.at("fox_vc", 0))
                            pe.wait_ge(S["fox_c"], st.at("fox_c", 0))
                            pe.wait_ge(S["fox_q"], st.at("fox_q", 0))
                            pe.wait_ge(S["pool_t"], st.at("pool_t", 0))
                        if st.at("ao_copied", 0):
                            pe.wait_ge(S["ao_copied"], st.at("ao_copied", 0))
                        U = st.heads * st.nq
                        groups = all_groups(st)
                        for u in range(U + 2):
                            if u < U:
                                hd, qt = unit(st, u)
                                n = n_keys(st, qt)
                                if u >= 2:
                                    pe.wait_ge(S["p_exp"], st.at("p_exp", u - 1))
                                for c0 in range(0, n, BANK):
                                    c1 = min(n, c0 + BANK)
                                    dst = ps[:, 2 * (u % 2) * BANK + c0:2 * (u % 2) * BANK + c1]
                                    if st.first:
                                        half, r = hd % 2, 64 * (hd % 2)
                                        kv = hd // 4
                                        kk = k_all if kv == half else k_swap
                                        q = zt(hd // 2, st.s)[r:r + 64, qt * P:(qt + 1) * P]
                                        mm = nc.tensor.matmul(dst, q, kk[r:r + 64, c0:c1], start=True, stop=True)
                                    elif hd < MLA_H:
                                        nc.tensor.matmul(dst, mla_qt[hd][0:MLA_D, qt * P:(qt + 1) * P],
                                                         mla_kt[hd][0:MLA_D, c0:c1], start=True, stop=False)
                                        mm = nc.tensor.matmul(dst[:, n - P:n], ident, konst[:, K_MASK:K_MASK + P],
                                                              start=False, stop=True)
                                    else:
                                        f = hd - MLA_H
                                        r = 64 * (f % 2)
                                        nc.tensor.matmul(dst, zt(5 + f // 2)[r:r + 64, qt * P:(qt + 1) * P],
                                                         zt(8 + f // 2)[r:r + 64, c0:c1], start=True, stop=False)
                                        nc.tensor.matmul(dst, konst[0:FOX_H, f:f + 1].to_broadcast([FOX_H, P]),
                                                         zt(15)[0:FOX_H, c0:c1], start=False, stop=False)
                                        mm = nc.tensor.matmul(dst[:, n - P:n], ident, konst[:, K_MASK:K_MASK + P],
                                                              start=False, stop=True)
                                mm.then_inc(S["s_ready"], 1)
                            if u >= 2 and unit(st, u - 2)[1] == st.nq - 1:
                                hd = unit(st, u - 2)[0]
                                done = [i for i, (v, _) in enumerate(groups) if v <= u - 2]
                                n_act = sum(on_act(i) for i in done)
                                if n_act:
                                    pe.wait_ge(S["pt_act"], st.at("pt_act", n_act))
                                pe.wait_ge(S["pt_dve"], st.at("pt_dve", len(done) - n_act))
                                if hd >= 2:
                                    pe.wait_ge(S["ao_copied"], st.at("ao_copied", hd - 1))
                                nk = n_keys(st, st.nq - 1) // P
                                for kt in range(nk):
                                    q0 = 0 if st.first else kt * P
                                    if st.first:
                                        v = v_all[:, kt, 64 * (hd // 4):64 * (hd // 4) + 64]
                                    elif hd < MLA_H:
                                        v = v_mla[:, kt, 64 * hd:64 * hd + 64]
                                    else:
                                        f = hd - MLA_H
                                        v = zt(11 + f // 2)[:, kt * P + 64 * (f % 2):kt * P + 64 * (f % 2) + 64]
                                    mm = nc.tensor.matmul(bank(6 + hd % 2)[0:64, q0:st.nq * P], v,
                                                          att_pt(st, kt, q0, st.nq * P), start=(kt == 0), stop=(kt == nk - 1))
                                mm.then_inc(S["pv_done"], 1)
                            if 1 <= u <= U:
                                pe.wait_ge(S["p_norm"], st.at("p_norm", u))
                                for i, (v, kts) in enumerate(groups):
                                    if v != u - 1:
                                        continue
                                    if i >= 2:
                                        if on_act(i - 2):
                                            pe.wait_ge(S["pt_act"], st.at("pt_act", (i - 2) // 2 + 1))
                                        else:
                                            pe.wait_ge(S["pt_dve"], st.at("pt_dve", (i - 2) // 2 + 1))
                                    for j, kt in enumerate(kts):
                                        mm = nc.tensor.transpose(bank(4 + i % 2)[:, j * P:(j + 1) * P],
                                                                 att_p(st, (u - 1) % 2, n_keys(st, unit(st, u - 1)[1])
                                                                       )[:, kt * P:(kt + 1) * P], ident)
                                    mm.then_inc(S["p_turned"], 1)
                    elif st.kind == "mixer2":
                        pe.wait_ge(S["z_taken"], st.at("z_taken", 0))
                        pe.wait_ge(S["mla_sq"], st.at("mla_sq", 3))
                        for k in range(2):
                            mm = nc.tensor.matmul(bank(4), konst[:, K_AVG256:K_AVG256 + P], mla_sq[k],
                                                  start=(k == 0), stop=(k == 1))
                        mm.then_inc(S["mla_ms"], 1)
                        nc.tensor.matmul(bank(5), konst[:, K_AVG128:K_AVG128 + P], mla_sq[2], start=True, stop=True
                                         ).then_inc(S["mla_ms"], 1)
                        for j in range(3):
                            if j == 2:
                                pe.wait_ge(S["fox_vc"], st.at("fox_vc", 1))
                            for t in range(TT):
                                mm = nc.tensor.transpose(bank(j % 2)[:, t * P:(t + 1) * P],
                                                         zt(11 + j)[:, t * P:(t + 1) * P], ident)
                            mm.then_inc(S["fox_vt"], 1)
                        pe.wait_ge(S["bd_loaded"], st.at("bd_loaded", 64))
                        for j in range(2):
                            pe.wait_ge(S["pool_m"], st.at("pool_m", j + 1))
                            nc.tensor.matmul(bank(2 + j), pool_bd[:, j, :], zt(3 + j), start=True, stop=True
                                             ).then_inc(S["pool_y"], 1)
                        pe.wait_ge(S["mla_loaded"], st.at("mla_loaded", 32))
                        pe.wait_ge(S["mla_n"], st.at("mla_n", 3))
                        pe.wait_ge(S["fox_vc"], st.at("fox_vc", 3))
                        nc.tensor.matmul(bank(6)[0:MLA_D, :], konst[0:MLA_D, K_ROTM:K_ROTM + MLA_D], zt(14)[0:MLA_D, :],
                                         start=True, stop=True).then_inc(S["mla_rot"], 1)
                        for t in range(TT):
                            if t >= 2:
                                pe.wait_ge(S["mla_vc"], st.at("mla_vc", t - 1))
                            nc.tensor.matmul(bank(4 + t % 2, 384), zt(2)[:, t * P:(t + 1) * P],
                                             wkv_b.rearrange("p (h a f) -> p h a f", h=MLA_H, a=2)[:, :, 1, :],
                                             start=True, stop=True).then_inc(S["mla_v"], 1)
                        def rot_q(hd):
                            pe.wait_ge(S["mla_qc"], st.at("mla_qc", hd + 1))
                            pe.wait_ge(S["mla_qf"], st.at("mla_qf", hd + 1))
                            nc.tensor.matmul(bank(6)[0:MLA_D, :], konst[0:MLA_D, K_ROTM:K_ROTM + MLA_D],
                                             mla_qt[hd][0:MLA_D, :], start=True, stop=True).then_inc(S["mla_rot"], 1)
                        for hd in range(MLA_H):
                            if hd >= 2:
                                pe.wait_ge(S["mla_qc"], st.at("mla_qc", hd - 1))
                                pe.wait_ge(S["mla_kc"], st.at("mla_kc", 2 * (hd - 2) + 1))
                            for k in range(2):
                                mm = nc.tensor.matmul(bank(hd % 2)[0:MLA_D, :], wq_b[:, k, hd * MLA_D:(hd + 1) * MLA_D], zt(k),
                                                      start=(k == 0), stop=(k == 1))
                            mm.then_inc(S["mla_q"], 1)
                            if hd == 0:
                                pe.wait_ge(S["pool_t"], st.at("pool_t", 2))
                                pe.wait_ge(S["mla_vc"], st.at("mla_vc", 4))
                            nc.tensor.matmul(bank(2 + hd % 2)[0:64, :], wkv_b[:, hd * P:hd * P + 64], zt(2),
                                             start=True, stop=True).then_inc(S["mla_k"], 1)
                            if hd >= 1:
                                rot_q(hd - 1)
                        rot_q(MLA_H - 1)
                    elif st.kind == "store":
                        for t in range(TT):
                            for half in range(2):
                                i = 2 * t + half
                                if i == 0:
                                    pe.wait_ge(S["y_ready"], KD)
                                if i >= 4:
                                    pe.wait_ge(S["y_copied"], i - 3)
                                for j in range(4):
                                    mm = nc.tensor.transpose(bank(i % 4)[:, j * P:(j + 1) * P],
                                                             x_lat[:, 4 * half + j, t * P:(t + 1) * P], ident)
                                mm.then_inc(S["y_turned"], 1)

            @block.scalar
            def _(act):
                def split(g, slot, kt):
                    if kt is None:
                        return
                    if not isinstance(g, int) or g >= 2:
                        act.wait_ge(S["chunk_done"], g - 1)
                    turn = turns(g, slot)
                    act.wait_ge(w_loaded[slot], turn)
                    nc.scalar.activation(w_hi_sb[:, slot, 0:kt * P], w_raw[:, slot, 0:kt * P], ACT.Copy
                                         ).then_inc(S["w_hi"], 1)

                def turns(g, slot):
                    return (g + (2 - slot)) * 8

                def root(dst, src):
                    return nc.scalar.activation(dst, src, ACT.Sqrt, bias=eps_col[:, 0:1])

                def hi_copy(dst, src, bias=None):
                    if bias is None:
                        return nc.scalar.activation(dst, src, ACT.Copy)
                    return nc.scalar.activation(dst, src, ACT.Identity, bias=bias)

                for st in stages:
                    if st.kind == "setup":
                        for i in range(2 * (TT + CT)):
                            act.wait_ge(S["x_turned"], i + 1)
                            t, k0 = i // 2, 4 * (i % 2)
                            dst = x_lat[:, k0:k0 + 4, t * P:(t + 1) * P] if t < TT else \
                                x_ctx[:, k0:k0 + 4, (t - TT) * P:(t - TT + 1) * P]
                            nc.scalar.activation(dst, bank(i % 4).rearrange("p (j t) -> p j t", j=4), ACT.Copy
                                                 ).then_inc(S["x_copied"], 1)
                        act.wait_ge(S["rows_turned"], 1)
                        nc.scalar.activation(pc[:], bank(4, P), ACT.Copy).then_inc(S["rows_copied"], 1)
                        nc.scalar.activation(bmod[:], bank(5, 96), ACT.Copy).then_inc(S["rows_copied"], 1)
                        nc.scalar.activation(silu_c[:].rearrange("p s k -> p (s k)"), bank(4)[:, R_C:R_C + 16], ACT.Silu
                                             ).then_inc(S["silu_done"], 1)
                        for g in range(2):
                            split(g, g, KD)
                    elif st.kind == "norm":
                        act.wait_ge(S["sum_ready"], st.at("sum_ready", 1))
                        for s in st.sets:
                            o = root(norm_rs[s], bank({"lat": 0, "ctx": 4}[s], W[s]))
                        o.then_inc(S["root_ready"], 1)
                        for i, (m, s) in enumerate([(m, s) for m in range(KD) for s in st.sets]):
                            if st.to_h:
                                act.wait_ge(S["norm_t"], st.at("norm_t", i + 1))
                                hi_copy(HH[s][:, m, :], norm_tmp[i % 2][:, 0:W[s]], st.b_col(s, m)
                                        ).then_inc(S["h_hi"], 1)
                    elif st.kind in ("linear_z", "linear_z2"):
                        def take(c, nkt, func, sets):
                            for s in range(2):
                                split(c + (st.chunk0 + 2 + s), s, nkt)
                                act.wait_ge(S["chunk_done"], c + (st.chunk0 + s + 1))
                                for i, name in enumerate(sets):
                                    base = (14 * T if name == "ctx" else 0)
                                    o = nc.scalar.activation(z[:, bass.ds((c + s) * W[name] + base, W[name])],
                                                             bank({"lat": 0, "ctx": 4}[name] + s, W[name]), func)
                                o.then_inc(S["z_taken"], 1)
                        if st.kind == "linear_z":
                            more = st.more
                            if more == st.sets:
                                with act.Fori(0, 3) as i:
                                    take(i * 2, KD, ACT.Copy, more)
                            else:
                                with act.Fori(0, 2) as i:
                                    take(i * 2, KD, ACT.Copy, more)
                                take(4, KD, ACT.Copy, st.sets)
                            with act.Fori(3, 6) as i:
                                take(i * 2, KD, ACT.Gelu_apprx_tanh, more)
                            take(12, next_kt(st), ACT.Gelu_apprx_tanh, more)
                        else:
                            chunk_pairs(act, st, lambda c, nkt: take(c, nkt, ACT.Copy, st.sets))
                    elif st.kind == "linear_r":
                        def pair(c, nkt):
                            for s in range(2):
                                split(c + (st.chunk0 + 2 + s), s, nkt)
                        chunk_pairs(act, st, pair)
                    elif st.kind == "linear_sqrelu":
                        def pair(c, nkt):
                            for s in range(2):
                                split(c + (st.chunk0 + 2 + s), s, nkt)
                                act.wait_ge(S["chunk_done"], c + (st.chunk0 + s + 1))
                                act.wait_ge(S["t_ready"], c + (st.at("t_ready", 0) + s - 1))
                                for name in st.sets:
                                    o = nc.scalar.activation(ff_r[name][s], bank({"lat": 0, "ctx": 4}[name] + s, W[name]),
                                                             ACT.Relu)
                                o.then_inc(S["relu_ready"], 1)
                                act.wait_ge(S["t_ready"], c + (st.at("t_ready", 0) + s + 1))
                                for name in st.sets:
                                    dst = m1h_lat if name == "lat" else m1h_ctx
                                    o = hi_copy(dst[:, tile_ds(c + s), :].rearrange("p a t -> p (a t)"), ff_t[name][s])
                                o.then_inc(S["mid_hi"], 1)
                        chunk_pairs(act, st, pair)
                    elif st.kind == "linear_glu":
                        def pair(i, nkt):
                            g0 = i * 2 + st.chunk0
                            split(g0 + 2, 0, nkt)
                            act.wait_ge(S["chunk_done"], g0 + 1)
                            act.wait_ge(S["t_ready"], i + st.at("t_ready", 0))
                            nc.scalar.activation(ff_silu, bank(0), ACT.Silu).then_inc(S["silu_taken"], 1)
                            split(g0 + 3, 1, nkt)
                            act.wait_ge(S["t_ready"], i + st.at("t_ready", 1))
                            hi_copy(m2h[:, tile_ds(i), :].rearrange("p a t -> p (a t)"), ff_t["lat"][0]).then_inc(S["mid_hi"], 1)
                        with act.Fori(0, FG - 1) as i:
                            pair(i, KD)
                        pair(FG - 1, next_kt(st))
                    elif st.kind == "spatial":
                        act.wait_ge(S["ws_turned"], st.at("ws_turned", 1))
                        nc.scalar.activation(ws_t.rearrange("p g q -> p (g q)"), bank(6), ACT.Copy
                                             ).then_inc(S["ws_copied"], 1)
                        i = 0
                        n_t = 0
                        for s in st.sets:
                            for t in range(W[s] // P):
                                n_t += 1
                                act.wait_ge(S["g_var"], st.at("g_var", n_t))
                                nc.scalar.activation(grs[:], grs[:], ACT.Sqrt).then_inc(S["g_root"], 1)
                            for g in range(4):
                                act.wait_ge(S["gm_t"], st.at("gm_t", i + 1))
                                hi_copy(HH[s][:, 4 + g, :], gm_tmp[i % 2][:, 0:W[s]]).then_inc(S["gm_hi"], 1)
                                i += 1
                    elif st.kind == "qk_heads":
                        items = qk_items(st)
                        for i in range(len(items) + 1):
                            if i < len(items):
                                s, tile = items[i]
                                if i >= 2:
                                    act.wait_ge(S["q_ms"], st.at("q_ms", i - 1))
                                nc.scalar.activation(qk_sq[i % 2][:, 0:W[s]], zt(tile, s), ACT.Square
                                                     ).then_inc(S["q_sq"], 1)
                            if i >= 1:
                                s = items[i - 1][0]
                                act.wait_ge(S["q_ms"], st.at("q_ms", i))
                                if i >= 3:
                                    act.wait_ge(S["q_n"], st.at("q_n", i - 2))
                                root(qk_rs[(i - 1) % 2][:, 0:W[s]], bank((i - 1) % 2, W[s])).then_inc(S["q_root"], 1)
                        act.wait_ge(S["v_turned"], st.at("v_turned", 1))
                        nc.scalar.activation(v_all[:, 2:6, :].rearrange("p t f -> p (t f)"), bank(4), ACT.Copy)
                        nc.scalar.activation(v_all[:, 0:2, :].rearrange("p t f -> p (t f)"), bank(5, C), ACT.Copy
                                             ).then_inc(S["v_copied"], 1)
                        act.wait_ge(S["q_fin"], st.at("q_fin", 1))
                        act.wait_ge(S["q_n"], st.at("q_n", 2))
                        nc.scalar.activation(k_swap[64:128, :], k_all[0:64, :], ACT.Copy)
                        nc.scalar.activation(k_swap[0:64, :], k_all[64:128, :], ACT.Copy).then_inc(S["k_dup"], 1)
                    elif st.kind == "attention":
                        U = st.heads * st.nq
                        groups = all_groups(st)
                        for u in range(U + 2):
                            if u < U:
                                n = n_keys(st, unit(st, u)[1])
                                act.wait_ge(S["s_max"], st.at("s_max", u + 1))
                                if u >= 2:
                                    done = sum(v <= u - 2 for v, _ in groups)
                                    act.wait_ge(S["p_turned"], st.at("p_turned", done))
                                nc.scalar.activation(att_p(st, u % 2, n), ps[:, 2 * (u % 2) * BANK:2 * (u % 2) * BANK + n],
                                                     ACT.Exp, bias=nmax[:, u % 2:u % 2 + 1],
                                                     accum_out=rsum[:, u % 2:u % 2 + 1]).then_inc(S["p_exp"], 1)
                            if u >= 2:
                                hd, qt = unit(st, u - 2)
                                for i, (v, kts) in enumerate(groups):
                                    if v == u - 2 and on_act(i):
                                        act.wait_ge(S["p_turned"], st.at("p_turned", i + 1))
                                        nc.scalar.activation(pt_dst(st, kts, qt), pt_src(i, kts), ACT.Copy
                                                             ).then_inc(S["pt_act"], 1)
                                if qt == st.nq - 1:
                                    n = st.nq * P
                                    r = 64 * (hd % 2)
                                    act.wait_ge(S["pv_done"], st.at("pv_done", hd + 1))
                                    if hd % 2 == 0 and st.at("ao_lo", hd // 2):
                                        act.wait_ge(S["ao_lo"], st.at("ao_lo", hd // 2))
                                    nc.scalar.activation(att_out(st, n)[r:r + 64, :], bank(6 + hd % 2)[0:64, 0:n], ACT.Copy
                                                         ).then_inc(S["ao_copied"], 1)
                                    if hd % 2 == 1:
                                        act.wait_ge(S["ao_copied"], st.at("ao_copied", hd + 1))
                                        hi_copy(HH[st.s][:, out_tile(st, hd), :], att_out(st, n)).then_inc(S["ao_hi"], 1)
                    elif st.kind == "mixer2":
                        for j in range(3):
                            nc.scalar.activation(zt(5 + j), zt(5 + j), ACT.Copy, scale=HD ** -0.5).then_inc(S["fox_q"], 1)
                        for k in range(3):
                            nc.scalar.activation(mla_sq[k], zt(k), ACT.Square).then_inc(S["mla_sq"], 1)
                        for k in range(2):
                            act.wait_ge(S["mla_ms"], st.at("mla_ms", k + 1))
                            root(mla_rs[k], bank(4 + k)).then_inc(S["mla_root"], 1)
                        for j in range(3):
                            act.wait_ge(S["fox_vt"], st.at("fox_vt", j + 1))
                            nc.scalar.activation(zt(11 + j), bank(j % 2), ACT.Copy).then_inc(S["fox_vc"], 1)
                        act.wait_ge(S["fox_a"], st.at("fox_a", 1))
                        nc.scalar.activation(fox_t[2], fox_t[1], ACT.Exp).then_inc(S["fox_e"], 1)
                        act.wait_ge(S["fox_e"], st.at("fox_e", 1))
                        nc.scalar.activation(fox_t[3], fox_t[2], ACT.Ln, bias=1.0).then_inc(S["fox_e"], 1)
                        for j in range(2):
                            act.wait_ge(S["pool_t"], st.at("pool_t", j + 1))
                            hi_copy(hh_lat[:, 3 + j, :], pool_tmps[j]).then_inc(S["pool_hi"], 1)
                        for t in range(TT):
                            act.wait_ge(S["mla_v"], st.at("mla_v", t + 1))
                            nc.scalar.activation(v_mla[:, t, :], bank(4 + t % 2, 384), ACT.Copy).then_inc(S["mla_vc"], 1)
                        act.wait_ge(S["pool_lo"], st.at("pool_lo", 2))
                        act.wait_ge(S["fox_c"], st.at("fox_c", 1))
                        for hd in range(MLA_H):
                            act.wait_ge(S["mla_q"], st.at("mla_q", hd + 1))
                            nc.scalar.activation(mla_qt[hd][0:MLA_D, :], bank(hd % 2)[0:MLA_D, :], ACT.Copy,
                                                 scale=1.0 / math.sqrt(MLA_D)).then_inc(S["mla_qc"], 1)
                            act.wait_ge(S["mla_k"], st.at("mla_k", hd + 1))
                            nc.scalar.activation(mla_kt[hd][0:64, :], bank(2 + hd % 2)[0:64, :], ACT.Copy
                                                 ).then_inc(S["mla_kc"], 1)
                            if hd == 0:
                                act.wait_ge(S["mla_qf"], st.at("mla_qf", 1))
                            nc.scalar.activation(mla_kt[hd][64:96, :], zt(14)[64:96, :], ACT.Copy).then_inc(S["mla_kc"], 1)
                    elif st.kind == "store":
                        for i in range(2 * TT):
                            act.wait_ge(S["y_turned"], i + 1)
                            nc.scalar.activation(z[:, 4096 + i * 512:4096 + (i + 1) * 512], bank(i % 4), ACT.Copy
                                                 ).then_inc(S["y_copied"], 1)

            @block.vector
            def _(dve):
                chain = [0]

                def link(ins):
                    chain[0] += 1
                    ins.then_inc(S["dve_chain"], 1)
                    dve.wait_ge(S["dve_chain"], chain[0])

                def split(g, slot, kt):
                    if kt is None:
                        return
                    dve.wait_ge(S["w_hi"], g + 1)
                    nc.vector.tensor_tensor(w_lo_sb[:, slot, 0:kt * P], w_raw[:, slot, 0:kt * P],
                                            w_hi_sb[:, slot, 0:kt * P].bitcast(F32), ALU.subtract).then_inc(S["w_lo"], 1)

                def low(dst, src, hi):
                    return nc.vector.tensor_tensor(dst, src, hi.bitcast(F32), ALU.subtract)

                for st in stages:
                    if st.kind == "setup":
                        nc.vector.memset(eps_col[:], EPS)
                        nc.vector.memset(zero_col[:], 0.0).then_inc(S["r_taken"], 2)
                        nc.vector.memset(nmax[:], 0.0).then_inc(S["t_ready"], 2)
                        nc.vector.memset(rsum[:], 0.0).then_inc(S["relu_ready"], 2)
                        nc.vector.memset(rinv[:], 0.0).then_inc(S["mid_lo"], 2)
                        for g in range(2):
                            split(g, g, KD)
                        dve.wait_ge(S["rows_copied"], 2)
                        link(nc.vector.tensor_scalar(pc[:, R_QK:R_QK + 2], pc[:, R_QK:R_QK + 2], HD ** -0.5, None, ALU.mult))
                    elif st.kind == "mod":
                        for l in range(L):
                            with dve.Fori(0, 6) as i:
                                for n in range(2):
                                    dve.wait_ge(S["mod_used"], i * 4 + (24 * l + 2 * n + 2))
                                    nc.vector.tensor_tensor(
                                        modv[:, l, bass.ds(i * 8 + 4 * n, 4), :],
                                        bank(6 + n, 8).rearrange("p (m c) -> p m c", c=2),
                                        bmod[:, bass.ds(i * 8 + (48 * l + 4 * n), 4)].unsqueeze(2).to_broadcast([P, 4, 2]),
                                        ALU.add).then_inc(S["mod_taken"], 1)
                        dve.wait_ge(S["mod_taken"], 24)
                        for l in range(L):
                            for i in range(2):
                                r = (R_N1 if i == 0 else R_N2) + KD * l
                                for c in range(2):
                                    o = nc.vector.scalar_tensor_tensor(
                                        gains[:, l, i, c, :], modv[:, l, 24 * i + 8:24 * i + 16, c], 1.0, pc[:, r:r + KD],
                                        ALU.add, ALU.mult)
                        link(o)
                    elif st.kind == "norm":
                        dve.wait_ge(S["root_ready"], st.at("root_ready", 1))
                        for s in st.sets:
                            o = nc.vector.reciprocal(norm_rs[s], norm_rs[s])
                        o.then_inc(S["rstd_ready"], 1)
                        dve.wait_ge(S["rstd_ready"], st.at("rstd_ready", 1))
                        items = [(m, s) for m in range(KD) for s in st.sets]

                        def lower(i):
                            m, s = items[i]
                            dve.wait_ge(S["h_hi"], st.at("h_hi", i + 1))
                            nc.vector.scalar_tensor_tensor(HL[s][:, m, :], norm_tmp[i % 2][:, 0:W[s]], st.b_col(s, m),
                                                           HH[s][:, m, :].bitcast(F32), ALU.add, ALU.subtract
                                                           ).then_inc(S["h_lo"], 1)
                        for i, (m, s) in enumerate(items):
                            if st.to_h:
                                if i >= 2:
                                    dve.wait_ge(S["h_lo"], st.at("h_lo", i - 1))
                                nc.vector.scalar_tensor_tensor(norm_tmp[i % 2][:, 0:W[s]], X[s][:, m, :], st.a_col(s, m),
                                                               norm_rs[s], ALU.mult, ALU.mult).then_inc(S["norm_t"], 1)
                                if i >= 1:
                                    lower(i - 1)
                            else:
                                nc.vector.scalar_tensor_tensor(X[s][:, m, :], X[s][:, m, :], st.a_col(s, m),
                                                               norm_rs[s], ALU.mult, ALU.mult).then_inc(S["y_ready"], 1)
                        if st.to_h:
                            lower(len(items) - 1)
                    elif st.kind in ("linear_z", "linear_z2"):
                        def pair(c, nkt):
                            for s in range(2):
                                split(c + (st.chunk0 + 2 + s), s, nkt)
                        chunk_pairs(dve, st, pair)
                    elif st.kind == "linear_r":
                        def pair(c, nkt):
                            for s in range(2):
                                split(c + (st.chunk0 + 2 + s), s, nkt)
                                dve.wait_ge(S["chunk_done"], c + (st.chunk0 + s + 1))
                                dve.wait_ge(S["r_taken"], c + (st.at("r_taken", 0) + s - 1))
                                for name in st.sets:
                                    x = X[name][:, tile_ds(c + s), :].rearrange("p a t -> p (a t)")
                                    o = nc.vector.scalar_tensor_tensor(
                                        x, bank({"lat": 2, "ctx": 6}[name] + s, W[name]), st.gate(name, c + s), x,
                                        ALU.mult, ALU.add)
                                o.then_inc(S["r_taken"], 1)
                        chunk_pairs(dve, st, pair)
                    elif st.kind == "linear_sqrelu":
                        def pair(c, nkt):
                            for s in range(2):
                                split(c + (st.chunk0 + 2 + s), s, nkt)
                                dve.wait_ge(S["relu_ready"], c + (st.at("relu_ready", 0) + s + 1))
                                dve.wait_ge(S["mid_lo"], c + (st.at("mid_lo", 0) + s - 1))
                                for name in st.sets:
                                    o = nc.vector.tensor_tensor(ff_t[name][s], ff_r[name][s], ff_r[name][s], ALU.mult)
                                o.then_inc(S["t_ready"], 1)
                                dve.wait_ge(S["mid_hi"], c + (st.at("mid_hi", 0) + s + 1))
                                for name in st.sets:
                                    hi, lo = (m1h_lat, m1l_lat) if name == "lat" else (m1h_ctx, m1l_ctx)
                                    o = low(lo[:, tile_ds(c + s), :].rearrange("p a t -> p (a t)"), ff_t[name][s],
                                            hi[:, tile_ds(c + s), :].rearrange("p a t -> p (a t)"))
                                o.then_inc(S["mid_lo"], 1)
                        chunk_pairs(dve, st, pair)
                    elif st.kind == "linear_glu":
                        def pair(i, nkt):
                            g0 = i * 2 + st.chunk0
                            split(g0 + 2, 0, nkt)
                            split(g0 + 3, 1, nkt)
                            dve.wait_ge(S["silu_taken"], i + st.at("silu_taken", 1))
                            dve.wait_ge(S["chunk_done"], g0 + 2)
                            dve.wait_ge(S["mid_lo"], i + st.at("mid_lo", 0))
                            nc.vector.tensor_tensor(ff_t["lat"][0], bank(1), ff_silu, ALU.mult).then_inc(S["t_ready"], 1)
                            dve.wait_ge(S["mid_hi"], i + st.at("mid_hi", 1))
                            low(m2l[:, tile_ds(i), :].rearrange("p a t -> p (a t)"), ff_t["lat"][0],
                                m2h[:, tile_ds(i), :].rearrange("p a t -> p (a t)")).then_inc(S["mid_lo"], 1)
                        with dve.Fori(0, FG - 1) as i:
                            pair(i, KD)
                        pair(FG - 1, next_kt(st))
                    elif st.kind == "spatial":
                        tiles = [(s, t) for s in st.sets for t in range(W[s] // P)]
                        dve.wait_ge(S["ws_loaded"], st.at("ws_loaded", 80))
                        i = 0
                        n_t = 0
                        for i, (s, t) in enumerate(tiles):
                            dve.wait_ge(S["g_turned"], st.at("g_turned", i + 1))
                            b = bank(i % 2).rearrange("p (g c) -> p g c", g=4)
                            for g in range(4):
                                o = nc.vector.bn_stats(stats[:, g, :], b[:, g, :])
                            link(o)
                            for g in range(4):
                                o = nc.vector.bn_aggr(mv[:, g, :], stats[:, g, :])
                            link(o)
                            nc.vector.tensor_scalar(grs[:], mv[:, :, 1:2], EPS, None, ALU.add).then_inc(S["g_var"], 1)
                            dve.wait_ge(S["g_root"], st.at("g_root", i + 1))
                            link(nc.vector.reciprocal(grs[:], grs[:]))
                            for g in range(4):
                                o = nc.vector.tensor_scalar(zt(10 + g, s)[:, t * P:(t + 1) * P], b[:, g, :], mv[:, g, 0:1],
                                                            grs[:, g, :], ALU.subtract, ALU.mult)
                            o.then_inc(S["g_hat"], 1)
                            if t == W[s] // P - 1:
                                nt = W[s] // P
                                dve.wait_ge(S["g_mixed"], st.at("g_mixed", st.sets.index(s) + 1))

                                def lower(j, g):
                                    dve.wait_ge(S["gm_hi"], st.at("gm_hi", j + 1))
                                    low(HL[s][:, 4 + g, :], gm_tmp[j % 2][:, 0:W[s]], HH[s][:, 4 + g, :]
                                        ).then_inc(S["gm_lo"], 1)
                                for g in range(4):
                                    tmp = gm_tmp[n_t % 2][:, 0:W[s]]
                                    if n_t >= 2:
                                        dve.wait_ge(S["gm_lo"], st.at("gm_lo", n_t - 1))
                                    link(nc.vector.scalar_tensor_tensor(
                                        tmp.rearrange("p (t c) -> p t c", t=nt),
                                        bank(2 + g, W[s]).rearrange("p (t c) -> p t c", t=nt),
                                        pc[:, R_GM + 4 * st.l + g:R_GM + 4 * st.l + g + 1],
                                        ws_bias[:, g:g + 1, :].to_broadcast([P, nt, P]), ALU.mult, ALU.add))
                                    nc.vector.tensor_tensor(tmp, tmp, zt(6 + g, s), ALU.mult).then_inc(S["gm_t"], 1)
                                    if g >= 1:
                                        lower(n_t - 1, g - 1)
                                    n_t += 1
                                lower(n_t - 1, 3)
                    elif st.kind == "qk_heads":
                        items = qk_items(st)
                        dve.wait_ge(S["rope_loaded"], 16)

                        def norm(i):
                            s, tile = items[i]
                            dve.wait_ge(S["q_root"], st.at("q_root", i + 1))
                            rs = qk_rs[i % 2][:, 0:W[s]]
                            nc.vector.reciprocal(rs, rs).then_inc(S["q_rs"], 1)
                            dve.wait_ge(S["q_rs"], st.at("q_rs", i + 1))
                            r = (R_QK + 2 if tile == 4 else R_QK) + st.l
                            dst = k_part(s) if (tile == 4 and s == "ctx") else zt(tile, s)
                            nc.vector.scalar_tensor_tensor(dst, zt(tile, s), pc[:, r:r + 1], rs, ALU.mult, ALU.mult
                                                           ).then_inc(S["q_n"], 1)

                        def turn(i):
                            s, tile = items[i]
                            if s == "ctx":
                                return
                            n = sum(x == "lat" for x, _ in items[:i])
                            dve.wait_ge(S["q_rot"], st.at("q_rot", n + 1))
                            if n:
                                dve.wait_ge(S["q_fin"], st.at("q_fin", n))
                            link(nc.vector.tensor_tensor(qk_tb, bank(2 + n % 2), rope[:, 1, :], ALU.mult))
                            link(nc.vector.tensor_tensor(zt(tile), zt(tile), rope[:, 0, :], ALU.mult))
                            dst = k_part(s) if tile == 4 else zt(tile)
                            nc.vector.tensor_tensor(dst, zt(tile), qk_tb, ALU.add).then_inc(S["q_fin"], 1)
                        for i in range(len(items) + 1):
                            if i < len(items):
                                norm(i)
                            if i >= 1:
                                turn(i - 1)
                    elif st.kind == "attention":
                        U = st.heads * st.nq
                        groups = all_groups(st)
                        for u in range(U + 2):
                            if u < U:
                                n = n_keys(st, unit(st, u)[1])
                                dve.wait_ge(S["s_ready"], st.at("s_ready", u + 1))
                                nc.vector.tensor_reduce(nmax[:, u % 2:u % 2 + 1],
                                                        ps[:, 2 * (u % 2) * BANK:2 * (u % 2) * BANK + n], AX.X, ALU.max,
                                                        negate=True).then_inc(S["s_max"], 1)
                            if 1 <= u <= U:
                                v = u - 1
                                n = n_keys(st, unit(st, v)[1])
                                dve.wait_ge(S["p_exp"], st.at("p_exp", u))
                                link(nc.vector.reciprocal(rinv[:, v % 2:v % 2 + 1], rsum[:, v % 2:v % 2 + 1]))
                                pr = att_p(st, v % 2, n)
                                nc.vector.tensor_scalar(pr, pr, rinv[:, v % 2:v % 2 + 1], None, ALU.mult
                                                        ).then_inc(S["p_norm"], 1)
                            if u >= 2:
                                hd, qt = unit(st, u - 2)
                                for i, (v, kts) in enumerate(groups):
                                    if v == u - 2 and not on_act(i):
                                        dve.wait_ge(S["p_turned"], st.at("p_turned", i + 1))
                                        nc.vector.tensor_copy(pt_dst(st, kts, qt), pt_src(i, kts)).then_inc(S["pt_dve"], 1)
                            if u >= 3 or u == U + 1:
                                for w in ((u - 3, u - 2) if u == U + 1 else (u - 3,)):
                                    hd, qt = unit(st, w)
                                    if qt == st.nq - 1 and hd % 2 == 1:
                                        t = out_tile(st, hd)
                                        dve.wait_ge(S["ao_hi"], st.at("ao_hi", hd // 2 + 1))
                                        low(HL[st.s][:, t, :], att_out(st, st.nq * P), HH[st.s][:, t, :]
                                            ).then_inc(S["ao_lo"], 1)
                    elif st.kind == "mixer2":
                        dve.wait_ge(S["z_taken"], st.at("z_taken", 0))
                        u2 = z[:, 3 * T:5 * T].rearrange("p (j t) -> p j t", j=2)

                        def shifted(dst, src, w):
                            nc.vector.tensor_copy(dst[:, :, 0:w], src[:, :, 0:w])
                            link(nc.vector.tensor_tensor(dst[:, :, w:T], src[:, :, w:T], src[:, :, 0:T - w], ALU.add))
                        shifted(pool_a, u2, 1)
                        shifted(pool_b, pool_a, 2)
                        shifted(pool_a[:, 1:2, :], pool_b[:, 1:2, :], 4)
                        nc.vector.tensor_copy(pool_a[64:128, 0:1, :], pool_b[64:128, 0:1, :])
                        shifted(pool_b[64:128, 1:2, :], pool_a[64:128, 1:2, :], 8)
                        link(nc.vector.tensor_copy(pool_a[64:128, 1:2, :], pool_b[64:128, 1:2, :]))
                        link(nc.vector.tensor_tensor(pool_b[:, :, 0:16], pool_a[:, :, 0:16],
                                                     pool_k[:, 0:32].rearrange("p (j t) -> p j t", j=2), ALU.mult))
                        for j in range(2):
                            link(nc.vector.scalar_tensor_tensor(pool_a[:, j, 16:T], pool_a[:, j, 16:T],
                                                                pool_k[:, 32 + j:33 + j], u2[:, j, 16:T], ALU.mult,
                                                                ALU.subtract))
                            link(nc.vector.tensor_tensor(u2[:, j, 0:16], pool_b[:, j, 0:16], u2[:, j, 0:16], ALU.subtract))
                            nc.vector.tensor_copy(u2[:, j, 16:T], pool_a[:, j, 16:T]).then_inc(S["pool_m"], 1)
                        ft = zt(15)[0:FOX_H, :]
                        fb = pc[0:FOX_H, R_FB + st.l:R_FB + st.l + 1]
                        link(nc.vector.tensor_scalar(ft, ft, fb, None, ALU.add))
                        link(nc.vector.tensor_scalar(fox_t[0], ft, -1.0, None, ALU.mult))
                        nc.vector.tensor_tensor(fox_t[1], fox_t[0], ft, ALU.min).then_inc(S["fox_a"], 1)
                        dve.wait_ge(S["fox_a"], st.at("fox_a", 1))
                        link(nc.vector.tensor_scalar(fox_t[0], ft, 0.0, None, ALU.min))
                        dve.wait_ge(S["fox_e"], st.at("fox_e", 2))
                        link(nc.vector.tensor_tensor(fox_t[0], fox_t[3], fox_t[0], ALU.subtract))
                        dve.wait_ge(S["rope_loaded"], 32)
                        nc.vector.tensor_tensor_scan(ft, rope[0:FOX_H, 0, :], fox_t[0], 0.0, ALU.mult, ALU.add
                                                     ).then_inc(S["fox_c"], 1)
                        for j in range(2):
                            dve.wait_ge(S["pool_y"], st.at("pool_y", j + 1))
                            r = R_PS + 2 * st.l + j
                            nc.vector.tensor_scalar(pool_tmps[j], bank(2 + j), pc[:, r:r + 1], None, ALU.mult
                                                    ).then_inc(S["pool_t"], 1)
                        for j in range(2):
                            dve.wait_ge(S["pool_hi"], st.at("pool_hi", j + 1))
                            low(hl_lat[:, 3 + j, :], pool_tmps[j], hh_lat[:, 3 + j, :]).then_inc(S["pool_lo"], 1)
                        for k in range(2):
                            dve.wait_ge(S["mla_root"], st.at("mla_root", k + 1))
                            link(nc.vector.reciprocal(mla_rs[k], mla_rs[k]))
                        for k in range(3):
                            r = R_QA + 2 * st.l + k if k < 2 else R_KVA + st.l
                            nc.vector.scalar_tensor_tensor(zt(k), zt(k), pc[:, r:r + 1], mla_rs[0 if k < 2 else 1],
                                                           ALU.mult, ALU.mult).then_inc(S["mla_n"], 1)
                        for i in range(1 + MLA_H):
                            x = zt(14)[64:96, :] if i == 0 else mla_qt[i - 1][64:96, :]
                            dve.wait_ge(S["mla_rot"], st.at("mla_rot", i + 1))
                            if i:
                                dve.wait_ge(S["mla_qf"], st.at("mla_qf", i))
                            link(nc.vector.tensor_tensor(mla_tb[64:96, :], bank(6)[64:96, :], rope[64:96, 1, :], ALU.mult))
                            link(nc.vector.tensor_tensor(x, x, rope[64:96, 0, :], ALU.mult))
                            nc.vector.tensor_tensor(x, x, mla_tb[64:96, :], ALU.add).then_inc(S["mla_qf"], 1)

            @block.gpsimd
            def _(pool):
                chain = [0]

                def link(ins):
                    chain[0] += 1
                    ins.then_inc(S["pool_chain"], 1)
                    pool.wait_ge(S["pool_chain"], chain[0])

                def sum_squares(m, sets):
                    for s in sets:
                        if m == 0:
                            o = nc.gpsimd.tensor_tensor(sq_sum[s], X[s][:, 0, :], X[s][:, 0, :], ALU.mult)
                            continue
                        link(nc.gpsimd.tensor_tensor(sq_tmp[s], X[s][:, m, :], X[s][:, m, :], ALU.mult))
                        o = nc.gpsimd.tensor_tensor(sq_sum[s], sq_sum[s], sq_tmp[s], ALU.add)
                    return o

                nc.gpsimd.memset(z[:, 6 * D:6 * D + P], 0.0).then_inc(S["rows_zero"], 1)
                nc.gpsimd.memset(stats[:], 0.0).then_inc(S["z_taken"], 2)
                nc.gpsimd.memset(mv[:], 0.0).then_inc(S["silu_taken"], 1)
                pool.wait_ge(S["x_copied"], 2 * (TT + CT))
                for m in range(KD):
                    o = sum_squares(m, ("lat", "ctx"))
                    if m < KD - 1:
                        link(o)
                o.then_inc(S["sumsq"], 1)
                for st in stages:
                    if st.kind == "linear_r" and st.final:
                        for m in range(KD):
                            pool.wait_ge(S["r_taken"], st.at("r_taken", m + 1))
                            o = sum_squares(m, st.sets)
                            if m < KD - 1:
                                link(o)
                        o.then_inc(S["sumsq"], 1)
                    elif st.kind == "mixer2":
                        pool.wait_ge(S["chunk_done"], st.chunk0 - 1)
                        nc.gpsimd.memset(pool_bd.rearrange("p j m -> p (j m)"), 0.0).then_inc(S["bd_zero"], 1)


_INS = ["x", "c", "ctx", "c_ctx", "w_mod", "b_mod", "norm1_g", "w_in", "q_norm_g", "k_norm_g", "gmlp_norm_g",
        "w_spatial", "b_spatial", "w_out", "norm2_g", "w_ff1", "w_ff2", "ffn1_norm_2", "ffn1_w_gu_2",
        "ffn1_w_down_2", "mix_norm_2", "w_in_2", "q_a_norm_2", "w_q_b_2", "kv_a_norm_2", "w_kv_b_2", "pool_w_2",
        "pool_scale_2", "fox_b_f_2", "w_out_2", "ffn2_norm_2", "ffn2_w_gu_2", "ffn2_w_down_2", "final_norm_2"]


def kernel(**inputs):
    import concourse.bacc as bacc
    from concourse.bass_utils import run_bass_kernel_spmd as run

    nc = bacc.Bacc("TRN2", target_bir_lowering=False, num_devices=1)
    arrays, args = {}, {}
    for name in _INS:
        arr = np.ascontiguousarray(inputs[name])
        arrays[f"in_{name}"] = arr
        args[name] = nc.dram_tensor(f"in_{name}", arr.shape, mybir.dt.from_np(arr.dtype), kind="ExternalInput").ap()
    arrays["consts"] = shape_constants()
    args["consts"] = nc.dram_tensor("consts", arrays["consts"].shape, F32, kind="ExternalInput").ap()
    out = nc.dram_tensor("out_0", (1, T, D), F32, kind="ExternalOutput").ap()
    build_program(nc, args, out)
    r = run(nc, [arrays], core_ids=[0])
    return r.results[0]["out_0"]
```

```python
import math

import numpy as np

import concourse.bass as bass
from concourse import mybir

F32 = mybir.dt.float32
F32R = mybir.dt.float32r
ALU = mybir.AluOpType
ACT = mybir.ActivationFunctionType
AX = mybir.AxisListType

P = 128
D = 1024
KD = D // P
T = 512
C = 256
TT = T // P
CT = C // P
EPS = 1e-6
L = 2
HD = 64
FF1_GROUPS = 4
F2 = 2816
F2_TILES = F2 // P
F2_GROUPS = 2
FG = F2_TILES // F2_GROUPS
WMAX = FG * P
MLA_D = 96
MLA_H = 6
FOX_H = 6
BANK = 512
NEG = -1e38

K_IDENT, K_AVG_D, K_AVG256, K_AVG128, K_AVG64, K_ROT64, K_ROTM, K_MASK = [i * P for i in range(8)]
K_ROPE1 = 8 * P
K_ROPE2 = K_ROPE1 + 2 * T
K_POOL = K_ROPE2 + 2 * T
K_POOLW = K_POOL + 32
K_COLS = K_POOLW + 2


def shape_constants():
    f = np.float32
    t = np.zeros((P, K_COLS), f)
    t[:, K_IDENT:K_IDENT + P] = np.eye(P, dtype=f)
    t[:, K_AVG_D:K_AVG_D + P] = 1.0 / D
    t[:, K_AVG256:K_AVG256 + P] = 1.0 / 256
    t[:, K_AVG128:K_AVG128 + P] = 1.0 / 128
    t[:, K_AVG64:K_AVG64 + P] = np.kron(np.eye(2, dtype=f), np.full((HD, HD), 1.0 / HD, f))
    rot32 = np.zeros((32, 32), f)
    for i in range(16):
        rot32[i, 16 + i] = -1.0
        rot32[16 + i, i] = 1.0
    t[:, K_ROT64:K_ROT64 + P] = np.kron(np.eye(4, dtype=f), rot32).T
    rotm = np.zeros((P, P), f)
    rotm[64:96, 64:96] = rot32
    t[:, K_ROTM:K_ROTM + P] = rotm.T
    t[:, K_MASK:K_MASK + P] = np.where(np.arange(P)[None, :] <= np.arange(P)[:, None], f(0), f(NEG))
    freq = (f(10000.0) ** (-np.arange(16, dtype=f) / f(16))).astype(f)
    pos = np.arange(T, dtype=f)
    row = np.repeat(np.arange(T // 64, dtype=f), 64)
    col = np.tile(np.arange(64, dtype=f), T // 64)
    for p in range(P):
        ang = (row if (p % HD) < 32 else col) * freq[p % 16]
        t[p, K_ROPE1:K_ROPE1 + T] = np.cos(ang)
        t[p, K_ROPE1 + T:K_ROPE1 + 2 * T] = np.sin(ang)
    freq2 = (f(10000.0) ** (-np.arange(0, 32, 2, dtype=f) / f(32))).astype(f)
    t[:, K_ROPE2:K_ROPE2 + T] = 1.0
    for p in range(64, 96):
        ang = pos * freq2[p % 16]
        t[p, K_ROPE2:K_ROPE2 + T] = np.cos(ang)
        t[p, K_ROPE2 + T:K_ROPE2 + 2 * T] = np.sin(ang)
    for j in range(2):
        for half in range(2):
            w = 2 ** (2 * j + half + 1)
            rows = slice(64 * half, 64 * half + 64)
            t[rows, K_POOL + 16 * j:K_POOL + 16 * j + 16] = 1.0 / np.minimum(np.arange(1, 17), w).astype(f)
            t[rows, K_POOLW + j] = 1.0 / w
    return t


R_N1, R_N2, R_GM, R_F1, R_MX, R_F2, R_FIN, R_QA, R_KVA, R_PS, R_C, R_QK, R_FB = (
    0, 16, 32, 40, 56, 72, 88, 96, 100, 102, 106, 122, 126)


def build_program(nc, a, out):
    from contextlib import ExitStack
    ctx = ExitStack()
    with ctx:
        slab = ctx.enter_context(nc.sbuf_tensor("slab", [P, 53120], F32))
        at = [nc.sbuf_base - 53120 * 4]

        def place(name, shape, dt=F32, offset=None):
            size = 4 * int(np.prod(shape[1:]))
            where = at[0] if offset is None else offset
            t = nc.alloc_sbuf_tensor_at(name, shape, dt, offset=where)
            if offset is None:
                at[0] += -(-size // 32) * 32
                assert at[0] <= base0 + 53120 * 4, name
            return t

        base0 = at[0]
        x_lat = place("x_lat", [P, KD, T])
        x_ctx = place("x_ctx", [P, KD, C])
        hh_lat = place("hh_lat", [P, KD, T], F32R)
        hl_lat = place("hl_lat", [P, KD, T], F32R)
        hh_ctx = place("hh_ctx", [P, KD, C], F32R)
        hl_ctx = place("hl_ctx", [P, KD, C], F32R)
        mid0 = at[0]
        m1h_lat = place("m1h_lat", [P, 8, T], F32R)
        m1l_lat = place("m1l_lat", [P, 8, T], F32R)
        m1h_ctx = place("m1h_ctx", [P, 8, C], F32R)
        m1l_ctx = place("m1l_ctx", [P, 8, C], F32R)
        m2h = place("m2h", [P, FG, T], F32R, mid0)
        m2l = place("m2l", [P, FG, T], F32R, mid0 + FG * T * 4)
        scr = place("scr", [P, 12288], F32, mid0)
        z0 = at[0]
        z = place("z", [P, 14 * (T + C)])
        h2h = place("h2h", [P, KD, T], F32R, z0)
        h2l = place("h2l", [P, KD, T], F32R, z0 + KD * T * 4)
        w_raw = place("w_raw", [P, 2, WMAX])
        w_hi_sb = place("w_hi_sb", [P, 2, WMAX], F32R)
        w_lo_sb = place("w_lo_sb", [P, 2, WMAX], F32R)
        konst = place("konst", [P, 8 * P])
        rope = place("rope", [P, 2, T])
        pool_k = place("pool_k", [P, 34])
        pc = place("pc", [P, P])
        bmod = place("bmod", [P, 96])
        modv = place("modv", [P, L, 48, 2])
        gains = place("gains", [P, L, 2, 2, KD])
        silu_c = place("silu_c", [P, 2, KD])
        stats = place("stats", [P, 4, 6])
        mv = place("mv", [P, 4, 2])
        grs = place("grs", [P, 4, 1])
        nmax = place("nmax", [P, 2])
        rsum = place("rsum", [P, 2])
        rinv = place("rinv", [P, 2])
        zero_col = place("zero_col", [P, 1])
        eps_col = place("eps_col", [P, 1])
        table_out = place("table_out", [P, 32])
        marks = place("marks", [P, 8])
        ps = ctx.enter_context(nc.psum_tensor("ps", [P, 8 * BANK], F32))

        ident = konst[:, K_IDENT:K_IDENT + P]

        def bank(b, n=BANK):
            return ps[:, b * BANK:b * BANK + n]

        def zt(i, s="lat"):
            if s == "lat":
                return z[:, i * T:(i + 1) * T]
            return z[:, 14 * T + i * C:14 * T + (i + 1) * C]

        X = {"lat": x_lat, "ctx": x_ctx}
        HH = {"lat": hh_lat, "ctx": hh_ctx}
        HL = {"lat": hl_lat, "ctx": hl_ctx}
        W = {"lat": T, "ctx": C}

        names = ("w_hi w_lo chunk_done z_taken gate_taken up_taken silu_ready relu_ready t_ready mid_hi mid_lo r_taken "
                 "sumsq sum_ready root_ready rstd_ready norm_t h_hi h_lo "
                 "mod_used mod_taken mod_turned mod_added ws_turned ws_copied g_turned g_var g_root g_hat g_mixed gm_t gm_hi gm_lo "
                 "q_sq q_ms q_root q_rs q_n q_rot q_fin k_dup v_turned v_copied "
                 "s_ready s_max p_exp p_norm p_turned pt_act pt_dve pv_done ao_copied ao_hi ao_lo "
                 "mla_sq mla_ms mla_root mla_n mla_q mla_qc mla_rot mla_qf mla_k mla_kc mla_v mla_vc "
                 "fox_q fox_vt fox_vc fox_a fox_e fox_c bd_zero pool_m pool_y pool_t pool_hi pool_lo "
                 "rows_zero rows_turned rows_copied silu_done x_turned x_copied y_ready y_turned y_copied "
                 "dve_chain pool_chain").split()
        dma_names = ("w_loaded0 w_loaded1 mod_loaded0 mod_loaded1 mod_loaded2 konst_loaded rows_loaded "
                     "x_loaded rope_loaded ws_loaded mla_loaded bd_loaded stored").split()
        S = {n: ctx.enter_context(nc.semaphore(n)) for n in names + dma_names}
        w_loaded = [S["w_loaded0"], S["w_loaded1"]]
        mod_loaded = [S[f"mod_loaded{i}"] for i in range(3)]

        stages = []
        totals = {n: 0 for n in names + dma_names}
        for n in ("z_taken", "r_taken", "t_ready", "relu_ready", "mid_lo"):
            totals[n] = 2
        totals["gate_taken"] = totals["up_taken"] = totals["silu_ready"] = totals["h_lo"] = 1

        class Stage:
            def __init__(self, kind, counts, chunks=0, **spec):
                self.kind, self.spec = kind, spec
                self.chunk0 = sum(s.chunks for s in stages)
                self.chunks = chunks
                self.base = dict(totals)
                for n, k in counts.items():
                    totals[n] += k
                stages.append(self)

            def __getattr__(self, n):
                return self.spec[n]

            def at(self, name, k):
                return self.base[name] + k

        def add_norm(sets, a_col, b_col, to_h=True, block2=False):
            Stage("norm", dict(sum_ready=1, root_ready=1, rstd_ready=1, norm_t=KD * len(sets), h_hi=KD * len(sets),
                               h_lo=KD * len(sets)), sets=sets, a_col=a_col, b_col=b_col, to_h=to_h, block2=block2)

        def col(r):
            return lambda s, m: pc[:, r + m:r + m + 1]

        def no_shift(s, m):
            return zero_col[:, 0:1]

        Stage("setup", dict(sumsq=1))
        Stage("mod", {})
        for l in range(L):
            both = ("lat", "ctx")
            more = both if l < L - 1 else ("lat",)

            def a_col(i, l=l):
                return lambda s, m: gains[:, l, i, 0 if s == "lat" else 1, m:m + 1]

            def b_col(i, l=l):
                return lambda s, m: modv[:, l, 24 * i + m, (0 if s == "lat" else 1):(1 if s == "lat" else 2)]

            def gate(i, l=l):
                return lambda s, m: modv[:, l, bass.ds(24 * i + 16 + m, 1), 0 if s == "lat" else 1]

            add_norm(both, a_col(0), b_col(0))
            Stage("linear_z", dict(z_taken=14), 14, w="w_in", l=l, sets=both, more=more)
            Stage("spatial", dict(ws_turned=1, ws_copied=1, g_turned=TT + CT * (len(more) - 1), g_mixed=len(more),
                                  g_hat=TT + CT * (len(more) - 1), g_var=TT + CT * (len(more) - 1),
                                  g_root=TT + CT * (len(more) - 1), gm_t=4 * len(more), gm_hi=4 * len(more),
                                  gm_lo=4 * len(more), ws_loaded=80), l=l, sets=more)
            nqk = 5 + (5 if l < L - 1 else 1)
            Stage("qk_heads", dict(q_sq=nqk, q_ms=nqk, q_root=nqk, q_rs=nqk, q_n=nqk, q_rot=5, q_fin=5, k_dup=1, v_turned=1,
                                   v_copied=1), l=l, sets=more)
            for s in more[::-1]:
                nq = W[s] // P
                keys = C + T if s == "lat" else C
                U = 8 * nq
                groups = U * (2 if keys > BANK else 1)
                Stage("attention", dict(s_ready=U, s_max=U, p_exp=U, p_norm=U, p_turned=groups,
                                        pt_act=groups // 2, pt_dve=groups - groups // 2, pv_done=8, ao_copied=8,
                                        ao_hi=4, ao_lo=4), first=True, s=s, l=l, nq=nq, heads=8)
            Stage("linear_r", dict(r_taken=8, sumsq=1), 8, src="w_out", l=l, sets=more, gate=gate(0), group=None,
                  final=True, kt=KD, prep=None, block2=False)
            add_norm(more, a_col(1), b_col(1))
            for g in range(FF1_GROUPS):
                Stage("linear_sqrelu", dict(relu_ready=8, t_ready=8, mid_hi=8, mid_lo=8), 8, l=l, sets=more, group=g)
                last = g == FF1_GROUPS - 1
                ends = last and l == L - 1
                Stage("linear_r", dict(r_taken=8, sumsq=1 * last, norm_t=8 * ends, h_hi=8 * ends, h_lo=8 * ends), 8,
                      src="w_ff2", l=l, sets=more, gate=gate(1), group=g, final=last, kt=KD,
                      prep=(R_F1, hh_lat, hl_lat) if ends else None, block2=ends)
        lat = ("lat",)
        for l in range(L):
            def half(s, m):
                return 0.5

            def one(s, m):
                return 1.0

            for part in ("ffn1", "mix", "ffn2"):
                if part == "mix":
                    Stage("linear_z2", dict(z_taken=16, sum_ready=1, root_ready=1, rstd_ready=1), 16, l=l, sets=lat)
                    Stage("mixer2", dict(bd_zero=1, pool_m=2, pool_y=2, pool_t=2, pool_hi=2, pool_lo=2, fox_q=3, fox_vt=3,
                                         fox_vc=3, fox_a=1, fox_e=2, fox_c=1, mla_sq=3, mla_ms=2, mla_root=2, mla_n=3, mla_q=6,
                                         mla_qc=6, mla_rot=7, mla_qf=7, mla_k=6, mla_kc=12, mla_v=4, mla_vc=4,
                                         mla_loaded=32, bd_loaded=64), l=l)
                    U = 12 * TT
                    Stage("attention", dict(s_ready=U, s_max=U, p_exp=U, p_norm=U, p_turned=U, pt_act=U // 2,
                                            pt_dve=U - U // 2, pv_done=12, ao_copied=12, ao_hi=6, ao_lo=6),
                          first=False, s="lat", l=l, nq=TT, heads=12)
                    Stage("linear_r", dict(r_taken=8, sumsq=1, norm_t=8, h_hi=8, h_lo=8), 8, src="w_out_2", l=l, sets=lat,
                          gate=one, group=None, final=True, kt=KD, prep=(R_F2 + KD * l, h2h, h2l), block2=True)
                else:
                    for g in range(F2_GROUPS):
                        n1 = int(g == 0)
                        Stage("linear_glu", dict(gate_taken=FG, up_taken=FG, silu_ready=FG, t_ready=FG, mid_hi=FG, mid_lo=FG,
                                                 sum_ready=n1, root_ready=n1, rstd_ready=n1), 2 * FG, l=l, sets=lat,
                              group=g, part=part, x=(h2h, h2l) if part == "ffn2" else (hh_lat, hl_lat))
                        last = g == F2_GROUPS - 1
                        if part == "ffn1":
                            prep = (R_MX + KD * l, hh_lat, hl_lat)
                        else:
                            prep = (R_F1 + KD * (l + 1), hh_lat, hl_lat) if l < L - 1 else None
                        k = 8 * (last and prep is not None)
                        Stage("linear_r", dict(r_taken=8, sumsq=1 * last, norm_t=k, h_hi=k, h_lo=k), 8,
                              src=part + "_w_down_2", l=l, sets=lat, gate=half, group=g, final=last, kt=FG,
                              prep=prep if last else None, block2=True)
        add_norm(lat, col(R_FIN), no_shift, to_h=False, block2=True)
        Stage("store", dict(y_turned=TT, y_copied=2 * TT))
        linear = [s for s in stages if s.chunks]

        def kt_of(st):
            return st.spec.get("kt", KD)

        def next_kt(st):
            i = linear.index(st)
            return kt_of(linear[i + 1]) if i + 1 < len(linear) else None

        def chunk_pairs(eng, st, body):
            n = st.chunks // 2
            if n > 1:
                with eng.Fori(0, n - 1) as i:
                    body(i * 2, kt_of(st))
            body(st.chunks - 2, next_kt(st))

        def tile_ds(i):
            return bass.ds(i, 1)

        def tile_of(t, i):
            return t[:, bass.ds(i, 1), :].rearrange("p a t -> p (a t)")

        def mod_slot(n):
            return scr[:, n * 4096:(n + 1) * 4096].rearrange("p (k m) -> p k m", k=KD)

        mod_rows = z[0:2, 4096:4096 + 6 * D]

        ws_raw = scr[:, 0:512].rearrange("p (g q) -> p g q", g=4)
        ws_t = scr[:, 512:1024].rearrange("p (g q) -> p g q", g=4)
        ws_bias = scr[:, 1024:1536].rearrange("p (g q) -> p g q", g=4)
        gm_tmp = [scr[:, 1536 + 512 * i:2048 + 512 * i] for i in range(2)]
        qk_sq = [scr[:, 2560 + 512 * i:3072 + 512 * i] for i in range(2)]
        qk_rs = [scr[:, 3584 + 512 * i:4096 + 512 * i] for i in range(2)]
        qk_tb = scr[:, 4608:5120]
        k_all = scr[:, 5120:5888]
        k_swap = scr[:, 5888:6656]
        v_all = scr[:, 6656:7424].rearrange("p (t f) -> p t f", t=6)
        wq_b = scr[:, 0:1152].rearrange("p (k m) -> p k m", k=2)
        wkv_b = scr[:, 1152:1920]
        mla_kt = [scr[:, 1920 + 512 * i:2432 + 512 * i] for i in range(6)]
        mla_qt = [scr[:, 4992 + 512 * i:5504 + 512 * i] for i in range(6)]
        mla_sq = [scr[:, 8064 + 512 * i:8576 + 512 * i] for i in range(3)]
        mla_rs = [scr[:, 9600 + 512 * i:10112 + 512 * i] for i in range(2)]
        mla_tb = scr[:, 10624:11136]
        pool_bd = scr[:, 11136:11392].rearrange("p (j m) -> p j m", j=2)
        pool_a = scr[:, 1920:2944].rearrange("p (j t) -> p j t", j=2)
        pool_b = scr[:, 2944:3968].rearrange("p (j t) -> p j t", j=2)
        fox_t = [scr[0:FOX_H, 4992 + 512 * i:5504 + 512 * i] for i in range(4)]
        v_mla = z[:, 16 * T:16 * T + 4 * 384].rearrange("p (t f) -> p t f", t=4)

        def att_p(st, i, n):
            p0 = 7424 if st.first else 8064
            w = 768 if st.first else 512
            return scr[:, p0 + w * i:p0 + w * i + n]

        def att_pt(st, kt, c0, c1):
            p0 = 8960 if st.first else 9088
            return scr[:, p0 + 512 * kt + c0:p0 + 512 * kt + c1]

        def att_out(st, n):
            p0 = 0 if st.first else 11136
            return scr[:, p0:p0 + n]

        norm_rs = {"lat": scr[:, 0:512], "ctx": scr[:, 512:768]}
        norm_tmp = [scr[:, 768 + 512 * i:1280 + 512 * i] for i in range(2)]
        sq_tmp = {"lat": z[:, 0:512], "ctx": z[:, 512:768]}
        sq_sum = {"lat": z[:, 768:1280], "ctx": z[:, 1280:1536]}
        x_free = x_ctx[:].rearrange("p k t -> p (k t)")
        rstd2, sq_sum2 = x_free[:, 0:512], x_free[:, 512:1024]
        prep_tmp = [x_free[:, 1024:1536], x_free[:, 1536:2048]]
        glu_t, glu_silu, glu_gate, glu_up, sq_tmp2 = [z[:, 8192 + 512 * i:8704 + 512 * i] for i in range(5)]
        ff_t = {"lat": [z[:, 2048:2560], z[:, 2560:3072]], "ctx": [z[:, 3072:3328], z[:, 3328:3584]]}
        ff_r = {"lat": [z[:, 3584:4096], z[:, 4096:4608]], "ctx": [z[:, 4608:4864], z[:, 4864:5120]]}

        def n_keys(st, qt):
            if st.first:
                return C + T if st.s == "lat" else C
            return (qt + 1) * P

        def key_groups(st, qt):
            n = n_keys(st, qt) // P
            return [range(0, min(4, n))] + ([range(4, n)] if n > 4 else [])

        def unit(st, u):
            return u // st.nq, u % st.nq

        def all_groups(st):
            found = []
            for u in range(st.heads * st.nq):
                for kts in key_groups(st, unit(st, u)[1]):
                    found.append((u, kts))
            return found

        def on_act(i):
            return i % 2 == 1

        def qk_items(st):
            items = [("lat", 4), ("ctx", 4)] + [("lat", i) for i in range(4)]
            if "ctx" in st.sets:
                items += [("ctx", i) for i in range(4)]
            return items

        def k_part(s):
            return k_all[:, C:C + T] if s == "lat" else k_all[:, 0:C]

        pool_tmps = [scr[:, 3968:4480], scr[:, 4480:4992]]

        def pt_dst(st, kts, qt):
            p0 = 8960 if st.first else 9088
            n = len(kts)
            v = scr[:, p0 + 512 * kts[0]:p0 + 512 * (kts[0] + n)].rearrange("p (k q) -> p k q", q=512)
            return v[:, :, qt * P:(qt + 1) * P]

        def pt_src(i, kts):
            return bank(4 + i % 2, len(kts) * P).rearrange("p (k q) -> p k q", q=P)

        def out_tile(st, hd):
            if st.first:
                return hd // 2
            return hd // 2 if hd < MLA_H else 5 + (hd - MLA_H) // 2

        with nc.Block() as block:

            @block.sync
            def _(sp):
                def load_chunk(st, c, slot, kt, src):
                    g = c + st.chunk0
                    sp.wait_ge(S["w_lo"], g - 1)
                    width = src.shape[-1]
                    off = 64 if width == 32 else 0
                    dst = w_raw[:, slot, 0:kt * P].rearrange("p (k m) -> p k m", m=P)[:, :, off:off + width]
                    sp.dma_start(dst, src).then_inc(w_loaded[slot], 16)

                def rows_of(w, k0, kt):
                    return w[k0 * P:(k0 + kt) * P, :].rearrange("(k p) m -> p k m", p=P)

                def stream(st, kt, src_of):
                    with sp.Fori(1 if st.chunk0 == 0 else 0, st.chunks // 2) as i:
                        for slot in range(2):
                            load_chunk(st, i * 2 + slot, slot, kt, src_of(i * 2 + slot))

                for st in stages:
                    if st.kind == "setup":
                        sp.dma_start(konst[:], a["consts"][:, 0:8 * P]).then_inc(S["konst_loaded"], 16)
                        sp.dma_start(pool_k[:], a["consts"][:, K_POOL:K_POOL + 34]).then_inc(S["konst_loaded"], 16)
                        for t in range(TT):
                            sp.dma_start(z[:, t * D:(t + 1) * D], a["x"][0, t * P:(t + 1) * P, :]).then_inc(S["x_loaded"], 16)
                        for t in range(CT):
                            sp.dma_start(z[:, (TT + t) * D:(TT + t + 1) * D], a["ctx"][0, t * P:(t + 1) * P, :]
                                         ).then_inc(S["x_loaded"], 16)
                        rows = z[:, 6 * D:6 * D + P]
                        sp.wait_ge(S["rows_zero"], 1)

                        def put(r, ap, n, w=P, at_col=0):
                            sp.dma_start(rows[r:r + n, at_col:at_col + w], ap).then_inc(S["rows_loaded"], 16)

                        k8 = "l (k p) -> (l k) p"
                        put(R_N1, a["norm1_g"].rearrange(k8, p=P), 16)
                        put(R_N2, a["norm2_g"].rearrange(k8, p=P), 16)
                        put(R_GM, a["gmlp_norm_g"].rearrange(k8, p=P), 8)
                        put(R_F1, a["ffn1_norm_2"].rearrange(k8, p=P), 16)
                        put(R_MX, a["mix_norm_2"].rearrange(k8, p=P), 16)
                        put(R_F2, a["ffn2_norm_2"].rearrange(k8, p=P), 16)
                        put(R_FIN, a["final_norm_2"].rearrange("(k p) -> k p", p=P), 8)
                        put(R_QA, a["q_a_norm_2"].rearrange(k8, p=P), 4)
                        put(R_KVA, a["kv_a_norm_2"].rearrange(k8, p=P), 2)
                        put(R_PS, a["pool_scale_2"].rearrange(k8, p=P), 4)
                        put(R_C, a["c"].rearrange(k8, p=P), 8)
                        put(R_C + 8, a["c_ctx"].rearrange("(k p) -> k p", p=P), 8)
                        for half in range(2):
                            put(R_QK, a["q_norm_g"][:, :], 2, HD, HD * half)
                            put(R_QK + 2, a["k_norm_g"][:, :], 2, HD, HD * half)
                        put(R_FB, a["fox_b_f_2"][:, :], 2, FOX_H)
                        sp.dma_start(z[0:96, 6 * D + P:6 * D + 2 * P], a["b_mod"].rearrange(k8, p=P)
                                     ).then_inc(S["rows_loaded"], 16)
                        for slot in range(2):
                            sp.dma_start(w_raw[:, slot, 0:KD * P].rearrange("p (k m) -> p k m", m=P),
                                         rows_of(a["w_in"][0], 0, KD)[:, :, slot * P:(slot + 1) * P]
                                         ).then_inc(w_loaded[slot], 16)
                    elif st.kind == "mod":
                        for l in range(L):
                            src = a["w_mod"][l].rearrange("(k p) m -> p k m", p=P)
                            if l == 0:
                                for n in range(3):
                                    sp.dma_start(mod_slot(n), src[:, :, n * 512:(n + 1) * 512]).then_inc(mod_loaded[n], 16)
                            with sp.Fori(1 - l, 4) as i:
                                for n in range(3):
                                    sp.wait_ge(S["mod_used"], i * 3 + (l * 12 + n - 2))
                                    sp.dma_start(mod_slot(n), src[:, :, bass.ds(i * 1536 + n * 512, 512)]
                                                 ).then_inc(mod_loaded[n], 16)
                    elif st.kind == "linear_z":
                        if st.l == 0:
                            sp.dma_start(rope[:], a["consts"][:, K_ROPE1:K_ROPE1 + 2 * T].rearrange("p (a t) -> p a t", a=2)
                                         ).then_inc(S["rope_loaded"], 16)
                        w = rows_of(a["w_in"][st.l], 0, KD)
                        stream(st, KD, lambda c: w[:, :, bass.ds(c * P, P)])
                    elif st.kind == "linear_z2":
                        if st.l == 0:
                            sp.dma_start(rope[:], a["consts"][:, K_ROPE2:K_ROPE2 + 2 * T].rearrange("p (a t) -> p a t", a=2)
                                         ).then_inc(S["rope_loaded"], 16)
                        w = rows_of(a["w_in_2"][st.l], 0, KD)
                        for c, c0 in enumerate((0, 128, 256, 416)):
                            load_chunk(st, c, c % 2, KD, w[:, :, c0:c0 + P])
                        with sp.Fori(2, 7) as i:
                            for slot in range(2):
                                load_chunk(st, i * 2 + slot, slot, KD, w[:, :, bass.ds(i * 256 + (slot * P + 416 - 3 * P), P)])
                        load_chunk(st, 14, 0, KD, w[:, :, 384:416])
                        load_chunk(st, 15, 1, KD, w[:, :, 1824:1830])
                    elif st.kind == "linear_r":
                        w = a[st.src][st.l]
                        k0 = 0 if st.group is None else st.group * st.kt
                        w = rows_of(w, k0, st.kt)
                        stream(st, st.kt, lambda c: w[:, :, bass.ds(c * P, P)])
                    elif st.kind == "linear_sqrelu":
                        w = rows_of(a["w_ff1"][st.l], 0, KD)
                        stream(st, KD, lambda c: w[:, :, bass.ds((c + 8 * st.group) * P, P)])
                    elif st.kind == "linear_glu":
                        w = rows_of(a[st.part + "_w_gu_2"][st.l], 0, KD)
                        with sp.Fori(0, FG) as i:
                            for slot in range(2):
                                load_chunk(st, i * 2 + slot, slot, KD,
                                           w[:, :, bass.ds(i * P + (slot * F2 + st.group * FG * P), P)])
                    elif st.kind == "spatial":
                        sp.wait_ge(S["chunk_done"], st.chunk0 - 1)
                        sp.dma_start(ws_raw[:, :, :], a["w_spatial"][st.l].rearrange("g p q -> p g q")
                                     ).then_inc(S["ws_loaded"], 16)
                        for g in range(4):
                            sp.dma_start(ws_bias[:, g, :], a["b_spatial"][st.l, g:g + 1, :].to_broadcast([P, P])
                                         ).then_inc(S["ws_loaded"], 16)
                    elif st.kind == "mixer2":
                        sp.wait_ge(S["chunk_done"], st.chunk0 - 1)
                        sp.dma_start(wq_b[:, :, :], a["w_q_b_2"][st.l].rearrange("(k p) m -> p k m", p=P)
                                     ).then_inc(S["mla_loaded"], 16)
                        sp.dma_start(wkv_b[:, :], a["w_kv_b_2"][st.l]).then_inc(S["mla_loaded"], 16)
                        sp.wait_ge(S["bd_zero"], st.at("bd_zero", 1))
                        for g in range(4):
                            r = 64 * (g % 2)
                            sp.dma_start(pool_bd[r:r + 64, g // 2, r:r + 64], a["pool_w_2"][st.l, g]
                                         ).then_inc(S["bd_loaded"], 16)
                    elif st.kind == "store":
                        for t in range(TT):
                            sp.wait_ge(S["y_copied"], st.at("y_copied", 2 * (t + 1)))
                            sp.dma_start(out[0, t * P:(t + 1) * P, :], z[:, 4096 + t * D:4096 + (t + 1) * D]
                                         ).then_inc(S["stored"], 16)
                        sp.wait_ge(S["stored"], 16 * TT)

            @block.tensor
            def _(pe):
                def products(dst, wslot, kt, hi, lo, n, before=None):
                    for k in range(kt):
                        if before is not None:
                            before(k)
                        wh = w_hi_sb[:, wslot, k * P:(k + 1) * P]
                        wl = w_lo_sb[:, wslot, k * P:(k + 1) * P]
                        nc.tensor.matmul(dst, wl, hi[:, k, 0:n], start=(k == 0), stop=False)
                        nc.tensor.matmul(dst, wh, lo[:, k, 0:n], start=False, stop=False)
                        mm = nc.tensor.matmul(dst, wh, hi[:, k, 0:n], start=False, stop=(k == kt - 1))
                    return mm

                def norm_sum(st, banks):
                    pe.wait_ge(S["sumsq"], st.at("sumsq", 0))
                    for s in st.sets:
                        mm = nc.tensor.matmul(bank(banks[s], W[s]), konst[:, K_AVG_D:K_AVG_D + P],
                                              sq_sum2 if st.spec.get("block2", True) else sq_sum[s], start=True, stop=True)
                    mm.then_inc(S["sum_ready"], 1)

                def run_linear(st, free, banks, xs, splits=None, inputs=None, sums=False):
                    def pair(c, sets, first=False):
                        for s in range(2):
                            g = c + (st.chunk0 + s)
                            pe.wait_ge(S["w_lo"], g + 1)
                            free(c, s)
                            for i, name in enumerate(sets):
                                hi, lo = xs[name]
                                before = None
                                if first and s == 0:
                                    per, total = (len(sets), kt_of(st) * len(sets)) if inputs == "h_lo" else (1, kt_of(st))

                                    def before(k):
                                        pe.wait_ge(S[inputs], st.at(inputs, k * per + min(i, per - 1) + 1 - total))
                                mm = products(bank(banks[name] + s, W[name]), s, kt_of(st), hi, lo, W[name], before)
                            mm.then_inc(S["chunk_done"], 1)
                            if first and s == 0 and sums:
                                norm_sum(st, {"lat": 4})

                    for a0, a1, sets in splits or [(0, st.chunks, st.sets)]:
                        if a0 == 0 and inputs:
                            pair(0, sets, True)
                            a0 = 2
                        if a1 - a0 > 2:
                            with pe.Fori(a0 // 2, a1 // 2) as i:
                                pair(i * 2, sets)
                        elif a1 > a0:
                            pair(a0, sets)

                h = {s: (HH[s], HL[s]) for s in W}
                mid1 = {"lat": (m1h_lat, m1l_lat), "ctx": (m1h_ctx, m1l_ctx)}
                mid2 = {"lat": (m2h, m2l)}
                up_banks = {"lat": 0, "ctx": 4}
                down_banks = {"lat": 2, "ctx": 6}

                for st in stages:
                    if st.kind == "setup":
                        pe.wait_ge(S["konst_loaded"], 32)
                        pe.wait_ge(S["x_loaded"], 16 * (TT + CT))
                        for i in range(2 * (TT + CT)):
                            if i >= 4:
                                pe.wait_ge(S["x_copied"], i - 3)
                            for j in range(4):
                                k = 4 * (i % 2) + j
                                mm = nc.tensor.transpose(bank(i % 4)[:, j * P:(j + 1) * P],
                                                         z[:, (i // 2) * D + k * P:(i // 2) * D + (k + 1) * P], ident)
                            mm.then_inc(S["x_turned"], 1)
                        pe.wait_ge(S["rows_loaded"], 16 * 18)
                        nc.tensor.transpose(bank(4, P), z[:, 6 * D:6 * D + P], ident)
                        nc.tensor.transpose(bank(5, 96), z[0:96, 6 * D + P:6 * D + 2 * P], konst[0:96, 0:96]
                                            ).then_inc(S["rows_turned"], 1)
                    elif st.kind == "mod":
                        pe.wait_ge(S["silu_done"], 1)
                        for l in range(L):
                            def blocks(i, first):
                                for n in range(3):
                                    pe.wait_ge(mod_loaded[n], i * 16 + (64 * l + 16))
                                    if not first:
                                        pe.wait_ge(S["mod_taken"], i * 3 + (12 * l + n - 2))
                                    for k in range(KD):
                                        mm = nc.tensor.matmul(bank(5 + n)[0:2, :], silu_c[:, :, k], mod_slot(n)[:, k, :],
                                                              start=(k == 0), stop=(k == KD - 1))
                                    mm.then_inc(S["mod_used"], 1)
                            if l == 0:
                                blocks(0, True)
                            with pe.Fori(1 - l, 4) as i:
                                blocks(i, False)
                            pe.wait_ge(S["mod_taken"], 12 * (l + 1))
                            if l:
                                pe.wait_ge(S["mod_added"], l)
                            for m in range(48):
                                mm = nc.tensor.transpose(bank(4)[:, 2 * m:2 * m + 2], mod_rows[:, m * P:(m + 1) * P],
                                                         konst[0:2, 0:2])
                            mm.then_inc(S["mod_turned"], 1)
                        pe.wait_ge(S["mod_added"], L)
                    elif st.kind == "norm":
                        norm_sum(st, up_banks)
                    elif st.kind == "linear_z":
                        def free(c, s):
                            pe.wait_ge(S["z_taken"], c + (st.at("z_taken", 0) + s - 1))
                        if st.sets == st.more:
                            run_linear(st, free, up_banks, h, inputs="h_lo")
                        else:
                            pe.wait_ge(S["h_lo"], st.at("h_lo", 0))
                            run_linear(st, free, up_banks, h, [(0, 4, ("lat",)), (4, 6, st.sets), (6, 14, ("lat",))])
                    elif st.kind == "linear_z2":
                        run_linear(st, lambda c, s: pe.wait_ge(S["z_taken"], c + (st.at("z_taken", 0) + s - 1)), up_banks, h,
                                   inputs="h_lo", sums=True)
                    elif st.kind == "linear_sqrelu":
                        run_linear(st, lambda c, s: pe.wait_ge(S["relu_ready"], c + (st.at("relu_ready", 0) + s - 1)),
                                   up_banks, h, inputs="h_lo" if st.group == 0 else None)
                    elif st.kind == "linear_glu":
                        def free(c, s):
                            n = "gate_taken" if s == 0 else "up_taken"
                            pe.wait_ge(S[n], c // 2 + st.at(n, 0))
                        first = st.group == 0
                        run_linear(st, free, up_banks, {"lat": st.x}, inputs="h_lo" if first else None, sums=first)
                    elif st.kind == "linear_r":
                        if st.group is None:
                            pe.wait_ge(S["ao_lo"], st.at("ao_lo", 0))
                            if "w_out" == st.src:
                                pe.wait_ge(S["gm_lo"], st.at("gm_lo", 0))
                            else:
                                pe.wait_ge(S["pool_lo"], st.at("pool_lo", 0))
                            xs = h
                        else:
                            xs = mid1 if st.src == "w_ff2" else mid2
                        run_linear(st, lambda c, s: pe.wait_ge(S["r_taken"], c + (st.at("r_taken", 0) + s - 1)), down_banks, xs,
                                   inputs=None if st.group is None else "mid_lo")
                    elif st.kind == "spatial":
                        pe.wait_ge(S["ws_loaded"], st.at("ws_loaded", 80))
                        pe.wait_ge(S["z_taken"], st.at("z_taken", 0))
                        for g in range(4):
                            mm = nc.tensor.transpose(bank(6)[:, g * P:(g + 1) * P], ws_raw[:, g, :], ident)
                        mm.then_inc(S["ws_turned"], 1)
                        tiles = [(s, t) for s in st.sets for t in range(W[s] // P)]

                        def turn(i):
                            s, t = tiles[i]
                            if i >= 2:
                                pe.wait_ge(S["g_hat"], st.at("g_hat", i - 1))
                            for g in range(4):
                                mm = nc.tensor.transpose(bank(i % 2)[:, g * P:(g + 1) * P],
                                                         zt(10 + g, s)[:, t * P:(t + 1) * P], ident)
                            mm.then_inc(S["g_turned"], 1)
                        turn(0)
                        pe.wait_ge(S["ws_copied"], st.at("ws_copied", 1))
                        for i, (s, t) in enumerate(tiles):
                            if i + 1 < len(tiles):
                                turn(i + 1)
                            pe.wait_ge(S["g_hat"], st.at("g_hat", i + 1))
                            if i == TT:
                                pe.wait_ge(S["gm_t"], st.at("gm_t", 4))
                            for g in range(4):
                                mm = nc.tensor.matmul(bank(2 + g)[:, t * P:(t + 1) * P], zt(10 + g, s)[:, t * P:(t + 1) * P],
                                                      ws_t[:, g, :], start=True, stop=True)
                            if t == W[s] // P - 1:
                                mm.then_inc(S["g_mixed"], 1)
                    elif st.kind == "qk_heads":
                        pe.wait_ge(S["gm_t"], st.at("gm_t", 0))
                        pe.wait_ge(S["g_hat"], st.at("g_hat", 0))
                        for t in range(TT):
                            nc.tensor.transpose(bank(4)[:, t * P:(t + 1) * P], zt(5)[:, t * P:(t + 1) * P], ident)
                        for t in range(CT):
                            mm = nc.tensor.transpose(bank(5)[:, t * P:(t + 1) * P], zt(5, "ctx")[:, t * P:(t + 1) * P], ident)
                        mm.then_inc(S["v_turned"], 1)
                        items = qk_items(st)

                        def rot(i):
                            s, tile = items[i]
                            if s == "lat":
                                n = sum(x == "lat" for x, _ in items[:i])
                                pe.wait_ge(S["q_n"], st.at("q_n", i + 1))
                                if n >= 2:
                                    pe.wait_ge(S["q_fin"], st.at("q_fin", n - 1))
                                nc.tensor.matmul(bank(2 + n % 2), konst[:, K_ROT64:K_ROT64 + P], zt(tile),
                                                 start=True, stop=True).then_inc(S["q_rot"], 1)
                        for i, (s, tile) in enumerate(items):
                            pe.wait_ge(S["q_sq"], st.at("q_sq", i + 1))
                            if i >= 2:
                                pe.wait_ge(S["q_rs"], st.at("q_rs", i - 1))
                            nc.tensor.matmul(bank(i % 2, W[s]), konst[:, K_AVG64:K_AVG64 + P], qk_sq[i % 2][:, 0:W[s]],
                                             start=True, stop=True).then_inc(S["q_ms"], 1)
                            if i >= 1:
                                rot(i - 1)
                        rot(len(items) - 1)
                    elif st.kind == "attention":
                        if st.first:
                            pe.wait_ge(S["q_fin"], st.at("q_fin", 0))
                            pe.wait_ge(S["q_n"], st.at("q_n", 0))
                            pe.wait_ge(S["k_dup"], st.at("k_dup", 0))
                            pe.wait_ge(S["v_copied"], st.at("v_copied", 0))
                        else:
                            pe.wait_ge(S["mla_qf"], st.at("mla_qf", 0))
                            pe.wait_ge(S["mla_kc"], st.at("mla_kc", 0))
                            pe.wait_ge(S["mla_vc"], st.at("mla_vc", 0))
                            pe.wait_ge(S["fox_vc"], st.at("fox_vc", 0))
                            pe.wait_ge(S["fox_c"], st.at("fox_c", 0))
                            pe.wait_ge(S["fox_q"], st.at("fox_q", 0))
                            pe.wait_ge(S["pool_t"], st.at("pool_t", 0))
                        if st.at("ao_copied", 0):
                            pe.wait_ge(S["ao_copied"], st.at("ao_copied", 0))
                        U = st.heads * st.nq
                        groups = all_groups(st)
                        for u in range(U + 2):
                            if u < U:
                                hd, qt = unit(st, u)
                                n = n_keys(st, qt)
                                if u >= 2:
                                    pe.wait_ge(S["p_exp"], st.at("p_exp", u - 1))
                                for c0 in range(0, n, BANK):
                                    c1 = min(n, c0 + BANK)
                                    dst = ps[:, 2 * (u % 2) * BANK + c0:2 * (u % 2) * BANK + c1]
                                    if st.first:
                                        half, r = hd % 2, 64 * (hd % 2)
                                        kv = hd // 4
                                        kk = k_all if kv == half else k_swap
                                        q = zt(hd // 2, st.s)[r:r + 64, qt * P:(qt + 1) * P]
                                        mm = nc.tensor.matmul(dst, q, kk[r:r + 64, c0:c1], start=True, stop=True)
                                    elif hd < MLA_H:
                                        nc.tensor.matmul(dst, mla_qt[hd][0:MLA_D, qt * P:(qt + 1) * P],
                                                         mla_kt[hd][0:MLA_D, c0:c1], start=True, stop=False)
                                        mm = nc.tensor.matmul(dst[:, n - P:n], ident, konst[:, K_MASK:K_MASK + P],
                                                              start=False, stop=True)
                                    else:
                                        f = hd - MLA_H
                                        r = 64 * (f % 2)
                                        nc.tensor.matmul(dst, zt(5 + f // 2)[r:r + 64, qt * P:(qt + 1) * P],
                                                         zt(8 + f // 2)[r:r + 64, c0:c1], start=True, stop=False)
                                        nc.tensor.matmul(dst, konst[0:FOX_H, f:f + 1].to_broadcast([FOX_H, P]),
                                                         zt(15)[0:FOX_H, c0:c1], start=False, stop=False)
                                        mm = nc.tensor.matmul(dst[:, n - P:n], ident, konst[:, K_MASK:K_MASK + P],
                                                              start=False, stop=True)
                                mm.then_inc(S["s_ready"], 1)
                            if u >= 2 and unit(st, u - 2)[1] == st.nq - 1:
                                hd = unit(st, u - 2)[0]
                                done = [i for i, (v, _) in enumerate(groups) if v <= u - 2]
                                n_act = sum(on_act(i) for i in done)
                                if n_act:
                                    pe.wait_ge(S["pt_act"], st.at("pt_act", n_act))
                                pe.wait_ge(S["pt_dve"], st.at("pt_dve", len(done) - n_act))
                                if hd >= 2:
                                    pe.wait_ge(S["ao_copied"], st.at("ao_copied", hd - 1))
                                nk = n_keys(st, st.nq - 1) // P
                                for kt in range(nk):
                                    q0 = 0 if st.first else kt * P
                                    if st.first:
                                        v = v_all[:, kt, 64 * (hd // 4):64 * (hd // 4) + 64]
                                    elif hd < MLA_H:
                                        v = v_mla[:, kt, 64 * hd:64 * hd + 64]
                                    else:
                                        f = hd - MLA_H
                                        v = zt(11 + f // 2)[:, kt * P + 64 * (f % 2):kt * P + 64 * (f % 2) + 64]
                                    mm = nc.tensor.matmul(bank(6 + hd % 2)[0:64, q0:st.nq * P], v,
                                                          att_pt(st, kt, q0, st.nq * P), start=(kt == 0), stop=(kt == nk - 1))
                                mm.then_inc(S["pv_done"], 1)
                            if 1 <= u <= U:
                                pe.wait_ge(S["p_norm"], st.at("p_norm", u))
                                for i, (v, kts) in enumerate(groups):
                                    if v != u - 1:
                                        continue
                                    if i >= 2:
                                        if on_act(i - 2):
                                            pe.wait_ge(S["pt_act"], st.at("pt_act", (i - 2) // 2 + 1))
                                        else:
                                            pe.wait_ge(S["pt_dve"], st.at("pt_dve", (i - 2) // 2 + 1))
                                    for j, kt in enumerate(kts):
                                        mm = nc.tensor.transpose(bank(4 + i % 2)[:, j * P:(j + 1) * P],
                                                                 att_p(st, (u - 1) % 2, n_keys(st, unit(st, u - 1)[1])
                                                                       )[:, kt * P:(kt + 1) * P], ident)
                                    mm.then_inc(S["p_turned"], 1)
                    elif st.kind == "mixer2":
                        pe.wait_ge(S["z_taken"], st.at("z_taken", 0))
                        pe.wait_ge(S["mla_sq"], st.at("mla_sq", 3))
                        for k in range(2):
                            mm = nc.tensor.matmul(bank(4), konst[:, K_AVG256:K_AVG256 + P], mla_sq[k],
                                                  start=(k == 0), stop=(k == 1))
                        mm.then_inc(S["mla_ms"], 1)
                        nc.tensor.matmul(bank(5), konst[:, K_AVG128:K_AVG128 + P], mla_sq[2], start=True, stop=True
                                         ).then_inc(S["mla_ms"], 1)
                        for j in range(3):
                            if j == 2:
                                pe.wait_ge(S["fox_vc"], st.at("fox_vc", 1))
                            for t in range(TT):
                                mm = nc.tensor.transpose(bank(j % 2)[:, t * P:(t + 1) * P],
                                                         zt(11 + j)[:, t * P:(t + 1) * P], ident)
                            mm.then_inc(S["fox_vt"], 1)
                        pe.wait_ge(S["bd_loaded"], st.at("bd_loaded", 64))
                        for j in range(2):
                            pe.wait_ge(S["pool_m"], st.at("pool_m", j + 1))
                            nc.tensor.matmul(bank(2 + j), pool_bd[:, j, :], zt(3 + j), start=True, stop=True
                                             ).then_inc(S["pool_y"], 1)
                        pe.wait_ge(S["mla_loaded"], st.at("mla_loaded", 32))
                        pe.wait_ge(S["mla_n"], st.at("mla_n", 3))
                        pe.wait_ge(S["fox_vc"], st.at("fox_vc", 3))
                        nc.tensor.matmul(bank(6)[0:MLA_D, :], konst[0:MLA_D, K_ROTM:K_ROTM + MLA_D], zt(14)[0:MLA_D, :],
                                         start=True, stop=True).then_inc(S["mla_rot"], 1)
                        for t in range(TT):
                            if t >= 2:
                                pe.wait_ge(S["mla_vc"], st.at("mla_vc", t - 1))
                            nc.tensor.matmul(bank(4 + t % 2, 384), zt(2)[:, t * P:(t + 1) * P],
                                             wkv_b.rearrange("p (h a f) -> p h a f", h=MLA_H, a=2)[:, :, 1, :],
                                             start=True, stop=True).then_inc(S["mla_v"], 1)
                        def rot_q(hd):
                            pe.wait_ge(S["mla_qc"], st.at("mla_qc", hd + 1))
                            pe.wait_ge(S["mla_qf"], st.at("mla_qf", hd + 1))
                            nc.tensor.matmul(bank(6)[0:MLA_D, :], konst[0:MLA_D, K_ROTM:K_ROTM + MLA_D],
                                             mla_qt[hd][0:MLA_D, :], start=True, stop=True).then_inc(S["mla_rot"], 1)
                        for hd in range(MLA_H):
                            if hd >= 2:
                                pe.wait_ge(S["mla_qc"], st.at("mla_qc", hd - 1))
                                pe.wait_ge(S["mla_kc"], st.at("mla_kc", 2 * (hd - 2) + 1))
                            for k in range(2):
                                mm = nc.tensor.matmul(bank(hd % 2)[0:MLA_D, :], wq_b[:, k, hd * MLA_D:(hd + 1) * MLA_D], zt(k),
                                                      start=(k == 0), stop=(k == 1))
                            mm.then_inc(S["mla_q"], 1)
                            if hd == 0:
                                pe.wait_ge(S["pool_t"], st.at("pool_t", 2))
                                pe.wait_ge(S["mla_vc"], st.at("mla_vc", 4))
                            nc.tensor.matmul(bank(2 + hd % 2)[0:64, :], wkv_b[:, hd * P:hd * P + 64], zt(2),
                                             start=True, stop=True).then_inc(S["mla_k"], 1)
                            if hd >= 1:
                                rot_q(hd - 1)
                        rot_q(MLA_H - 1)
                    elif st.kind == "store":
                        for t in range(TT):
                            for half in range(2):
                                i = 2 * t + half
                                if i == 0:
                                    pe.wait_ge(S["y_ready"], KD)
                                if i >= 4:
                                    pe.wait_ge(S["y_copied"], i - 3)
                                for j in range(4):
                                    mm = nc.tensor.transpose(bank(i % 4)[:, j * P:(j + 1) * P],
                                                             x_lat[:, 4 * half + j, t * P:(t + 1) * P], ident)
                                mm.then_inc(S["y_turned"], 1)

            @block.scalar
            def _(act):
                def split(g, slot, kt):
                    if kt is None:
                        return
                    if not isinstance(g, int) or g >= 2:
                        act.wait_ge(S["chunk_done"], g - 1)
                    turn = turns(g, slot)
                    act.wait_ge(w_loaded[slot], turn)
                    nc.scalar.activation(w_hi_sb[:, slot, 0:kt * P], w_raw[:, slot, 0:kt * P], ACT.Copy
                                         ).then_inc(S["w_hi"], 1)

                def turns(g, slot):
                    return (g + (2 - slot)) * 8

                def root(dst, src):
                    return nc.scalar.activation(dst, src, ACT.Sqrt, bias=eps_col[:, 0:1])

                def deferred_root(st):
                    use_table(ACT.Sqrt)
                    act.wait_ge(S["sum_ready"], st.at("sum_ready", 1))
                    root(rstd2, bank(4)).then_inc(S["root_ready"], 1)

                table_cols = iter(range(32))

                def use_table(func):
                    c = next(table_cols)
                    nc.scalar.activation(table_out[:, c:c + 1], zero_col[:], func)

                def hi_copy(dst, src, bias=None):
                    if bias is None:
                        return nc.scalar.activation(dst, src, ACT.Copy)
                    return nc.scalar.activation(dst, src, ACT.Identity, bias=bias)

                for st in stages:
                    if st.kind == "setup":
                        act.wait_ge(S["r_taken"], 2)
                        for i in range(2 * (TT + CT)):
                            act.wait_ge(S["x_turned"], i + 1)
                            t, k0 = i // 2, 4 * (i % 2)
                            dst = x_lat[:, k0:k0 + 4, t * P:(t + 1) * P] if t < TT else \
                                x_ctx[:, k0:k0 + 4, (t - TT) * P:(t - TT + 1) * P]
                            nc.scalar.activation(dst, bank(i % 4).rearrange("p (j t) -> p j t", j=4), ACT.Copy
                                                 ).then_inc(S["x_copied"], 1)
                        act.wait_ge(S["rows_turned"], 1)
                        nc.scalar.activation(pc[:], bank(4, P), ACT.Copy).then_inc(S["rows_copied"], 1)
                        nc.scalar.activation(bmod[:], bank(5, 96), ACT.Copy).then_inc(S["rows_copied"], 1)
                        nc.scalar.activation(silu_c[:].rearrange("p s k -> p (s k)"), bank(4)[:, R_C:R_C + 16], ACT.Silu
                                             ).then_inc(S["silu_done"], 1)
                        for g in range(2):
                            split(g, g, KD)
                    elif st.kind == "norm":
                        use_table(ACT.Sqrt)
                        act.wait_ge(S["sum_ready"], st.at("sum_ready", 1))
                        for s in st.sets:
                            o = root(rstd2 if st.block2 else norm_rs[s], bank({"lat": 0, "ctx": 4}[s], W[s]))
                        o.then_inc(S["root_ready"], 1)
                        for i, (m, s) in enumerate([(m, s) for m in range(KD) for s in st.sets]):
                            if st.to_h:
                                act.wait_ge(S["norm_t"], st.at("norm_t", i + 1))
                                hi_copy(HH[s][:, m, :], norm_tmp[i % 2][:, 0:W[s]], st.b_col(s, m)
                                        ).then_inc(S["h_hi"], 1)
                    elif st.kind == "linear_z2":
                        deferred_root(st)

                        def pair(c, nkt):
                            for s in range(2):
                                split(c + (st.chunk0 + 2 + s), s, nkt)
                        chunk_pairs(act, st, pair)
                    elif st.kind == "linear_z":
                        def take(c, nkt, func, sets):
                            for s in range(2):
                                split(c + (st.chunk0 + 2 + s), s, nkt)
                                act.wait_ge(S["chunk_done"], c + (st.chunk0 + s + 1))
                                for i, name in enumerate(sets):
                                    base = (14 * T if name == "ctx" else 0)
                                    o = nc.scalar.activation(z[:, bass.ds((c + s) * W[name] + base, W[name])],
                                                             bank({"lat": 0, "ctx": 4}[name] + s, W[name]), func)
                                o.then_inc(S["z_taken"], 1)
                        more = st.more
                        use_table(ACT.Gelu_apprx_tanh)
                        if more == st.sets:
                            with act.Fori(0, 3) as i:
                                take(i * 2, KD, ACT.Copy, more)
                        else:
                            with act.Fori(0, 2) as i:
                                take(i * 2, KD, ACT.Copy, more)
                            take(4, KD, ACT.Copy, st.sets)
                        with act.Fori(3, 6) as i:
                            take(i * 2, KD, ACT.Gelu_apprx_tanh, more)
                        take(12, next_kt(st), ACT.Gelu_apprx_tanh, more)
                    elif st.kind == "linear_r":
                        def pair(c, nkt):
                            for s in range(2):
                                split(c + (st.chunk0 + 2 + s), s, nkt)
                                if st.prep:
                                    act.wait_ge(S["norm_t"], c + (st.at("norm_t", 0) + s + 1))
                                    hi_copy(tile_of(st.prep[1], c + s), prep_tmp[s]).then_inc(S["h_hi"], 1)
                        chunk_pairs(act, st, pair)
                    elif st.kind == "linear_sqrelu":
                        def pair(c, nkt):
                            for s in range(2):
                                split(c + (st.chunk0 + 2 + s), s, nkt)
                                act.wait_ge(S["chunk_done"], c + (st.chunk0 + s + 1))
                                act.wait_ge(S["t_ready"], c + (st.at("t_ready", 0) + s - 1))
                                for name in st.sets:
                                    o = nc.scalar.activation(ff_r[name][s], bank({"lat": 0, "ctx": 4}[name] + s, W[name]),
                                                             ACT.Relu)
                                o.then_inc(S["relu_ready"], 1)
                                act.wait_ge(S["t_ready"], c + (st.at("t_ready", 0) + s + 1))
                                for name in st.sets:
                                    dst = m1h_lat if name == "lat" else m1h_ctx
                                    o = hi_copy(dst[:, tile_ds(c + s), :].rearrange("p a t -> p (a t)"), ff_t[name][s])
                                o.then_inc(S["mid_hi"], 1)
                        chunk_pairs(act, st, pair)
                    elif st.kind == "linear_glu":
                        if st.group == 0:
                            deferred_root(st)

                        def pair(i, nkt):
                            g0 = i * 2 + st.chunk0
                            split(g0 + 2, 0, nkt)
                            act.wait_ge(S["gate_taken"], i + st.at("gate_taken", 1))
                            act.wait_ge(S["t_ready"], i + st.at("t_ready", 0))
                            nc.scalar.activation(glu_silu, glu_gate, ACT.Silu).then_inc(S["silu_ready"], 1)
                            split(g0 + 3, 1, nkt)
                            act.wait_ge(S["t_ready"], i + st.at("t_ready", 1))
                            hi_copy(tile_of(m2h, i), glu_t).then_inc(S["mid_hi"], 1)
                        use_table(ACT.Silu)
                        with act.Fori(0, FG - 1) as i:
                            pair(i, KD)
                        pair(FG - 1, next_kt(st))
                    elif st.kind == "spatial":
                        act.wait_ge(S["ws_turned"], st.at("ws_turned", 1))
                        nc.scalar.activation(ws_t.rearrange("p g q -> p (g q)"), bank(6), ACT.Copy
                                             ).then_inc(S["ws_copied"], 1)
                        i = 0
                        n_t = 0
                        for s in st.sets:
                            for t in range(W[s] // P):
                                n_t += 1
                                act.wait_ge(S["g_var"], st.at("g_var", n_t))
                                nc.scalar.activation(grs[:], grs[:], ACT.Sqrt).then_inc(S["g_root"], 1)
                            for g in range(4):
                                act.wait_ge(S["gm_t"], st.at("gm_t", i + 1))
                                hi_copy(HH[s][:, 4 + g, :], gm_tmp[i % 2][:, 0:W[s]]).then_inc(S["gm_hi"], 1)
                                i += 1
                    elif st.kind == "qk_heads":
                        items = qk_items(st)
                        for i in range(len(items) + 1):
                            if i < len(items):
                                s, tile = items[i]
                                if i >= 2:
                                    act.wait_ge(S["q_ms"], st.at("q_ms", i - 1))
                                nc.scalar.activation(qk_sq[i % 2][:, 0:W[s]], zt(tile, s), ACT.Square
                                                     ).then_inc(S["q_sq"], 1)
                            if i >= 1:
                                s = items[i - 1][0]
                                act.wait_ge(S["q_ms"], st.at("q_ms", i))
                                if i >= 3:
                                    act.wait_ge(S["q_n"], st.at("q_n", i - 2))
                                root(qk_rs[(i - 1) % 2][:, 0:W[s]], bank((i - 1) % 2, W[s])).then_inc(S["q_root"], 1)
                        act.wait_ge(S["v_turned"], st.at("v_turned", 1))
                        nc.scalar.activation(v_all[:, 2:6, :].rearrange("p t f -> p (t f)"), bank(4), ACT.Copy)
                        nc.scalar.activation(v_all[:, 0:2, :].rearrange("p t f -> p (t f)"), bank(5, C), ACT.Copy
                                             ).then_inc(S["v_copied"], 1)
                        act.wait_ge(S["q_fin"], st.at("q_fin", 1))
                        act.wait_ge(S["q_n"], st.at("q_n", 2))
                        nc.scalar.activation(k_swap[64:128, :], k_all[0:64, :], ACT.Copy)
                        nc.scalar.activation(k_swap[0:64, :], k_all[64:128, :], ACT.Copy).then_inc(S["k_dup"], 1)
                    elif st.kind == "attention":
                        use_table(ACT.Exp)
                        U = st.heads * st.nq
                        groups = all_groups(st)
                        for u in range(U + 2):
                            if u >= 2:
                                hd, qt = unit(st, u - 2)
                                for i, (v, kts) in enumerate(groups):
                                    if v == u - 2 and on_act(i):
                                        act.wait_ge(S["p_turned"], st.at("p_turned", i + 1))
                                        nc.scalar.activation(pt_dst(st, kts, qt), pt_src(i, kts), ACT.Copy
                                                             ).then_inc(S["pt_act"], 1)
                            if u < U:
                                n = n_keys(st, unit(st, u)[1])
                                act.wait_ge(S["s_max"], st.at("s_max", u + 1))
                                if u >= 2:
                                    done = sum(v <= u - 2 for v, _ in groups)
                                    act.wait_ge(S["p_turned"], st.at("p_turned", done))
                                nc.scalar.activation(att_p(st, u % 2, n), ps[:, 2 * (u % 2) * BANK:2 * (u % 2) * BANK + n],
                                                     ACT.Exp, bias=nmax[:, u % 2:u % 2 + 1],
                                                     accum_out=rsum[:, u % 2:u % 2 + 1]).then_inc(S["p_exp"], 1)
                            if u >= 2:
                                hd, qt = unit(st, u - 2)
                                if qt == st.nq - 1:
                                    n = st.nq * P
                                    r = 64 * (hd % 2)
                                    act.wait_ge(S["pv_done"], st.at("pv_done", hd + 1))
                                    if hd % 2 == 0 and st.at("ao_lo", hd // 2):
                                        act.wait_ge(S["ao_lo"], st.at("ao_lo", hd // 2))
                                    nc.scalar.activation(att_out(st, n)[r:r + 64, :], bank(6 + hd % 2)[0:64, 0:n], ACT.Copy
                                                         ).then_inc(S["ao_copied"], 1)
                                    if hd % 2 == 1:
                                        act.wait_ge(S["ao_copied"], st.at("ao_copied", hd + 1))
                                        hi_copy(HH[st.s][:, out_tile(st, hd), :], att_out(st, n)).then_inc(S["ao_hi"], 1)
                    elif st.kind == "mixer2":
                        for j in range(3):
                            nc.scalar.activation(zt(5 + j), zt(5 + j), ACT.Copy, scale=HD ** -0.5).then_inc(S["fox_q"], 1)
                        for k in range(3):
                            nc.scalar.activation(mla_sq[k], zt(k), ACT.Square).then_inc(S["mla_sq"], 1)
                        for k in range(2):
                            act.wait_ge(S["mla_ms"], st.at("mla_ms", k + 1))
                            root(mla_rs[k], bank(4 + k)).then_inc(S["mla_root"], 1)
                        for j in range(3):
                            act.wait_ge(S["fox_vt"], st.at("fox_vt", j + 1))
                            nc.scalar.activation(zt(11 + j), bank(j % 2), ACT.Copy).then_inc(S["fox_vc"], 1)
                        act.wait_ge(S["fox_a"], st.at("fox_a", 1))
                        nc.scalar.activation(fox_t[2], fox_t[1], ACT.Exp).then_inc(S["fox_e"], 1)
                        act.wait_ge(S["fox_e"], st.at("fox_e", 1))
                        nc.scalar.activation(fox_t[3], fox_t[2], ACT.Ln, bias=1.0).then_inc(S["fox_e"], 1)
                        for j in range(2):
                            act.wait_ge(S["pool_t"], st.at("pool_t", j + 1))
                            hi_copy(hh_lat[:, 3 + j, :], pool_tmps[j]).then_inc(S["pool_hi"], 1)
                        for t in range(TT):
                            act.wait_ge(S["mla_v"], st.at("mla_v", t + 1))
                            nc.scalar.activation(v_mla[:, t, :], bank(4 + t % 2, 384), ACT.Copy).then_inc(S["mla_vc"], 1)
                        act.wait_ge(S["pool_lo"], st.at("pool_lo", 2))
                        act.wait_ge(S["fox_c"], st.at("fox_c", 1))
                        for hd in range(MLA_H):
                            act.wait_ge(S["mla_q"], st.at("mla_q", hd + 1))
                            nc.scalar.activation(mla_qt[hd][0:MLA_D, :], bank(hd % 2)[0:MLA_D, :], ACT.Copy,
                                                 scale=1.0 / math.sqrt(MLA_D)).then_inc(S["mla_qc"], 1)
                            act.wait_ge(S["mla_k"], st.at("mla_k", hd + 1))
                            nc.scalar.activation(mla_kt[hd][0:64, :], bank(2 + hd % 2)[0:64, :], ACT.Copy
                                                 ).then_inc(S["mla_kc"], 1)
                            if hd == 0:
                                act.wait_ge(S["mla_qf"], st.at("mla_qf", 1))
                            nc.scalar.activation(mla_kt[hd][64:96, :], zt(14)[64:96, :], ACT.Copy).then_inc(S["mla_kc"], 1)
                    elif st.kind == "store":
                        for i in range(2 * TT):
                            act.wait_ge(S["y_turned"], i + 1)
                            nc.scalar.activation(z[:, 4096 + i * 512:4096 + (i + 1) * 512], bank(i % 4), ACT.Copy
                                                 ).then_inc(S["y_copied"], 1)

            @block.vector
            def _(dve):
                chain = [0]

                def link(ins):
                    chain[0] += 1
                    ins.then_inc(S["dve_chain"], 1)
                    dve.wait_ge(S["dve_chain"], chain[0])

                def split(g, slot, kt):
                    if kt is None:
                        return
                    dve.wait_ge(S["w_hi"], g + 1)
                    nc.vector.tensor_tensor(w_lo_sb[:, slot, 0:kt * P], w_raw[:, slot, 0:kt * P],
                                            w_hi_sb[:, slot, 0:kt * P].bitcast(F32), ALU.subtract).then_inc(S["w_lo"], 1)

                def deferred_rstd(st):
                    dve.wait_ge(S["root_ready"], st.at("root_ready", 1))
                    nc.vector.reciprocal(rstd2, rstd2).then_inc(S["rstd_ready"], 1)
                    dve.wait_ge(S["rstd_ready"], st.at("rstd_ready", 1))

                def low(dst, src, hi):
                    return nc.vector.tensor_tensor(dst, src, hi.bitcast(F32), ALU.subtract)

                for st in stages:
                    if st.kind == "setup":
                        nc.vector.memset(eps_col[:], EPS)
                        nc.vector.memset(zero_col[:], 0.0).then_inc(S["r_taken"], 2)
                        nc.vector.memset(marks[:, 0:1], 0.0).then_inc(S["t_ready"], 2)
                        nc.vector.memset(marks[:, 1:2], 0.0).then_inc(S["relu_ready"], 2)
                        nc.vector.memset(marks[:, 2:3], 0.0).then_inc(S["mid_lo"], 2)
                        for g in range(2):
                            split(g, g, KD)
                        dve.wait_ge(S["rows_copied"], 2)
                        link(nc.vector.tensor_scalar(pc[:, R_QK:R_QK + 2], pc[:, R_QK:R_QK + 2], HD ** -0.5, None, ALU.mult))
                    elif st.kind == "mod":
                        for l in range(L):
                            if l:
                                dve.wait_ge(S["mod_turned"], l)
                            with dve.Fori(0, 4) as i:
                                for n in range(3):
                                    dve.wait_ge(S["mod_used"], i * 3 + (12 * l + n + 1))
                                    nc.vector.tensor_copy(mod_rows[:, bass.ds(i * 1536 + n * 512, 512)], bank(5 + n)[0:2, :]
                                                          ).then_inc(S["mod_taken"], 1)
                            dve.wait_ge(S["mod_turned"], l + 1)
                            nc.vector.tensor_tensor(modv[:, l, :, :], bank(4, 96).rearrange("p (m c) -> p m c", c=2),
                                                    bmod[:, 48 * l:48 * (l + 1)].unsqueeze(2).to_broadcast([P, 48, 2]),
                                                    ALU.add).then_inc(S["mod_added"], 1)
                        dve.wait_ge(S["mod_added"], L)
                        for l in range(L):
                            for i in range(2):
                                r = (R_N1 if i == 0 else R_N2) + KD * l
                                for c in range(2):
                                    o = nc.vector.scalar_tensor_tensor(
                                        gains[:, l, i, c, :], modv[:, l, 24 * i + 8:24 * i + 16, c], 1.0, pc[:, r:r + KD],
                                        ALU.add, ALU.mult)
                        link(o)
                    elif st.kind == "norm":
                        dve.wait_ge(S["root_ready"], st.at("root_ready", 1))
                        for s in st.sets:
                            rs = rstd2 if st.block2 else norm_rs[s]
                            o = nc.vector.reciprocal(rs, rs)
                        o.then_inc(S["rstd_ready"], 1)
                        dve.wait_ge(S["rstd_ready"], st.at("rstd_ready", 1))
                        items = [(m, s) for m in range(KD) for s in st.sets]

                        def lower(i):
                            m, s = items[i]
                            dve.wait_ge(S["h_hi"], st.at("h_hi", i + 1))
                            nc.vector.scalar_tensor_tensor(HL[s][:, m, :], norm_tmp[i % 2][:, 0:W[s]], st.b_col(s, m),
                                                           HH[s][:, m, :].bitcast(F32), ALU.add, ALU.subtract
                                                           ).then_inc(S["h_lo"], 1)
                        for i, (m, s) in enumerate(items):
                            if st.to_h:
                                if i >= 2:
                                    dve.wait_ge(S["h_lo"], st.at("h_lo", i - 1))
                                nc.vector.scalar_tensor_tensor(norm_tmp[i % 2][:, 0:W[s]], X[s][:, m, :], st.a_col(s, m),
                                                               norm_rs[s], ALU.mult, ALU.mult).then_inc(S["norm_t"], 1)
                                if i >= 1:
                                    lower(i - 1)
                            else:
                                nc.vector.scalar_tensor_tensor(X[s][:, m, :], X[s][:, m, :], st.a_col(s, m),
                                                               rstd2, ALU.mult, ALU.mult).then_inc(S["y_ready"], 1)
                        if st.to_h:
                            lower(len(items) - 1)
                    elif st.kind == "linear_z":
                        def pair(c, nkt):
                            for s in range(2):
                                split(c + (st.chunk0 + 2 + s), s, nkt)
                        chunk_pairs(dve, st, pair)
                    elif st.kind == "linear_z2":
                        deferred_rstd(st)

                        def pair(c, nkt):
                            for s in range(2):
                                split(c + (st.chunk0 + 2 + s), s, nkt)
                                dve.wait_ge(S["chunk_done"], c + (st.chunk0 + s + 1))
                                nc.vector.tensor_tensor(z[:, bass.ds((c + s) * T, T)], bank(s), rstd2, ALU.mult
                                                        ).then_inc(S["z_taken"], 1)
                        chunk_pairs(dve, st, pair)
                    elif st.kind == "linear_r":
                        def pair(c, nkt):
                            for s in range(2):
                                split(c + (st.chunk0 + 2 + s), s, nkt)
                                dve.wait_ge(S["chunk_done"], c + (st.chunk0 + s + 1))
                                dve.wait_ge(S["r_taken"], c + (st.at("r_taken", 0) + s - 1))
                                for name in st.sets:
                                    x = X[name][:, tile_ds(c + s), :].rearrange("p a t -> p (a t)")
                                    o = nc.vector.scalar_tensor_tensor(
                                        x, bank({"lat": 2, "ctx": 6}[name] + s, W[name]), st.gate(name, c + s), x,
                                        ALU.mult, ALU.add)
                                o.then_inc(S["r_taken"], 1)
                                if st.prep:
                                    r, hi, lo = st.prep
                                    dve.wait_ge(S["r_taken"], c + (st.at("r_taken", 0) + s + 1))
                                    dve.wait_ge(S["h_lo"], c + (st.at("h_lo", 0) + s))
                                    nc.vector.tensor_scalar(prep_tmp[s], tile_of(x_lat, c + s), pc[:, bass.ds(c + (r + s), 1)],
                                                            None, ALU.mult).then_inc(S["norm_t"], 1)
                                    dve.wait_ge(S["h_hi"], c + (st.at("h_hi", 0) + s + 1))
                                    low(tile_of(lo, c + s), prep_tmp[s], tile_of(hi, c + s)).then_inc(S["h_lo"], 1)
                        chunk_pairs(dve, st, pair)
                    elif st.kind == "linear_sqrelu":
                        def pair(c, nkt):
                            for s in range(2):
                                split(c + (st.chunk0 + 2 + s), s, nkt)
                                dve.wait_ge(S["relu_ready"], c + (st.at("relu_ready", 0) + s + 1))
                                dve.wait_ge(S["mid_lo"], c + (st.at("mid_lo", 0) + s - 1))
                                for name in st.sets:
                                    o = nc.vector.tensor_tensor(ff_t[name][s], ff_r[name][s], ff_r[name][s], ALU.mult)
                                o.then_inc(S["t_ready"], 1)
                                dve.wait_ge(S["mid_hi"], c + (st.at("mid_hi", 0) + s + 1))
                                for name in st.sets:
                                    hi, lo = (m1h_lat, m1l_lat) if name == "lat" else (m1h_ctx, m1l_ctx)
                                    o = low(lo[:, tile_ds(c + s), :].rearrange("p a t -> p (a t)"), ff_t[name][s],
                                            hi[:, tile_ds(c + s), :].rearrange("p a t -> p (a t)"))
                                o.then_inc(S["mid_lo"], 1)
                        chunk_pairs(dve, st, pair)
                    elif st.kind == "linear_glu":
                        if st.group == 0:
                            deferred_rstd(st)

                        def pair(i, nkt):
                            g0 = i * 2 + st.chunk0
                            split(g0 + 2, 0, nkt)
                            dve.wait_ge(S["chunk_done"], g0 + 1)
                            dve.wait_ge(S["silu_ready"], i + st.at("silu_ready", 0))
                            nc.vector.tensor_tensor(glu_gate, bank(0), rstd2, ALU.mult).then_inc(S["gate_taken"], 1)
                            split(g0 + 3, 1, nkt)
                            dve.wait_ge(S["chunk_done"], g0 + 2)
                            nc.vector.tensor_tensor(glu_up, bank(1), rstd2, ALU.mult).then_inc(S["up_taken"], 1)
                            dve.wait_ge(S["up_taken"], i + st.at("up_taken", 1))
                            dve.wait_ge(S["silu_ready"], i + st.at("silu_ready", 1))
                            dve.wait_ge(S["mid_lo"], i + st.at("mid_lo", 0))
                            nc.vector.tensor_tensor(glu_t, glu_up, glu_silu, ALU.mult).then_inc(S["t_ready"], 1)
                            dve.wait_ge(S["mid_hi"], i + st.at("mid_hi", 1))
                            low(tile_of(m2l, i), glu_t, tile_of(m2h, i)).then_inc(S["mid_lo"], 1)
                        with dve.Fori(0, FG - 1) as i:
                            pair(i, KD)
                        pair(FG - 1, next_kt(st))
                    elif st.kind == "spatial":
                        tiles = [(s, t) for s in st.sets for t in range(W[s] // P)]
                        dve.wait_ge(S["ws_loaded"], st.at("ws_loaded", 80))
                        i = 0
                        n_t = 0
                        for i, (s, t) in enumerate(tiles):
                            dve.wait_ge(S["g_turned"], st.at("g_turned", i + 1))
                            b = bank(i % 2).rearrange("p (g c) -> p g c", g=4)
                            for g in range(4):
                                o = nc.vector.bn_stats(stats[:, g, :], b[:, g, :])
                            link(o)
                            for g in range(4):
                                o = nc.vector.bn_aggr(mv[:, g, :], stats[:, g, :])
                            link(o)
                            nc.vector.tensor_scalar(grs[:], mv[:, :, 1:2], EPS, None, ALU.add).then_inc(S["g_var"], 1)
                            dve.wait_ge(S["g_root"], st.at("g_root", i + 1))
                            link(nc.vector.reciprocal(grs[:], grs[:]))
                            for g in range(4):
                                o = nc.vector.tensor_scalar(zt(10 + g, s)[:, t * P:(t + 1) * P], b[:, g, :], mv[:, g, 0:1],
                                                            grs[:, g, :], ALU.subtract, ALU.mult)
                            o.then_inc(S["g_hat"], 1)
                            if t == W[s] // P - 1:
                                nt = W[s] // P
                                dve.wait_ge(S["g_mixed"], st.at("g_mixed", st.sets.index(s) + 1))

                                def lower(j, g):
                                    dve.wait_ge(S["gm_hi"], st.at("gm_hi", j + 1))
                                    low(HL[s][:, 4 + g, :], gm_tmp[j % 2][:, 0:W[s]], HH[s][:, 4 + g, :]
                                        ).then_inc(S["gm_lo"], 1)
                                for g in range(4):
                                    tmp = gm_tmp[n_t % 2][:, 0:W[s]]
                                    if n_t >= 2:
                                        dve.wait_ge(S["gm_lo"], st.at("gm_lo", n_t - 1))
                                    link(nc.vector.scalar_tensor_tensor(
                                        tmp.rearrange("p (t c) -> p t c", t=nt),
                                        bank(2 + g, W[s]).rearrange("p (t c) -> p t c", t=nt),
                                        pc[:, R_GM + 4 * st.l + g:R_GM + 4 * st.l + g + 1],
                                        ws_bias[:, g:g + 1, :].to_broadcast([P, nt, P]), ALU.mult, ALU.add))
                                    nc.vector.tensor_tensor(tmp, tmp, zt(6 + g, s), ALU.mult).then_inc(S["gm_t"], 1)
                                    if g >= 1:
                                        lower(n_t - 1, g - 1)
                                    n_t += 1
                                lower(n_t - 1, 3)
                    elif st.kind == "qk_heads":
                        items = qk_items(st)
                        dve.wait_ge(S["rope_loaded"], 16)

                        def norm(i):
                            s, tile = items[i]
                            dve.wait_ge(S["q_root"], st.at("q_root", i + 1))
                            rs = qk_rs[i % 2][:, 0:W[s]]
                            nc.vector.reciprocal(rs, rs).then_inc(S["q_rs"], 1)
                            dve.wait_ge(S["q_rs"], st.at("q_rs", i + 1))
                            r = (R_QK + 2 if tile == 4 else R_QK) + st.l
                            dst = k_part(s) if (tile == 4 and s == "ctx") else zt(tile, s)
                            nc.vector.scalar_tensor_tensor(dst, zt(tile, s), pc[:, r:r + 1], rs, ALU.mult, ALU.mult
                                                           ).then_inc(S["q_n"], 1)

                        def turn(i):
                            s, tile = items[i]
                            if s == "ctx":
                                return
                            n = sum(x == "lat" for x, _ in items[:i])
                            dve.wait_ge(S["q_rot"], st.at("q_rot", n + 1))
                            if n:
                                dve.wait_ge(S["q_fin"], st.at("q_fin", n))
                            link(nc.vector.tensor_tensor(qk_tb, bank(2 + n % 2), rope[:, 1, :], ALU.mult))
                            link(nc.vector.tensor_tensor(zt(tile), zt(tile), rope[:, 0, :], ALU.mult))
                            dst = k_part(s) if tile == 4 else zt(tile)
                            nc.vector.tensor_tensor(dst, zt(tile), qk_tb, ALU.add).then_inc(S["q_fin"], 1)
                        for i in range(len(items) + 1):
                            if i < len(items):
                                norm(i)
                            if i >= 1:
                                turn(i - 1)
                    elif st.kind == "attention":
                        U = st.heads * st.nq
                        groups = all_groups(st)
                        for u in range(U + 2):
                            if u >= 2:
                                hd, qt = unit(st, u - 2)
                                for i, (v, kts) in enumerate(groups):
                                    if v == u - 2 and not on_act(i):
                                        dve.wait_ge(S["p_turned"], st.at("p_turned", i + 1))
                                        nc.vector.tensor_copy(pt_dst(st, kts, qt), pt_src(i, kts)).then_inc(S["pt_dve"], 1)
                            if 1 <= u <= U:
                                v = u - 1
                                n = n_keys(st, unit(st, v)[1])
                                dve.wait_ge(S["p_exp"], st.at("p_exp", u))
                                link(nc.vector.reciprocal(rinv[:, v % 2:v % 2 + 1], rsum[:, v % 2:v % 2 + 1]))
                                pr = att_p(st, v % 2, n)
                                nc.vector.tensor_scalar(pr, pr, rinv[:, v % 2:v % 2 + 1], None, ALU.mult
                                                        ).then_inc(S["p_norm"], 1)
                            if u < U:
                                n = n_keys(st, unit(st, u)[1])
                                dve.wait_ge(S["s_ready"], st.at("s_ready", u + 1))
                                nc.vector.tensor_reduce(nmax[:, u % 2:u % 2 + 1],
                                                        ps[:, 2 * (u % 2) * BANK:2 * (u % 2) * BANK + n], AX.X, ALU.max,
                                                        negate=True).then_inc(S["s_max"], 1)
                            if u >= 3 or u == U + 1:
                                for w in ((u - 3, u - 2) if u == U + 1 else (u - 3,)):
                                    hd, qt = unit(st, w)
                                    if qt == st.nq - 1 and hd % 2 == 1:
                                        t = out_tile(st, hd)
                                        dve.wait_ge(S["ao_hi"], st.at("ao_hi", hd // 2 + 1))
                                        low(HL[st.s][:, t, :], att_out(st, st.nq * P), HH[st.s][:, t, :]
                                            ).then_inc(S["ao_lo"], 1)
                    elif st.kind == "mixer2":
                        dve.wait_ge(S["z_taken"], st.at("z_taken", 0))
                        u2 = z[:, 3 * T:5 * T].rearrange("p (j t) -> p j t", j=2)

                        def shifted(dst, src, w):
                            nc.vector.tensor_copy(dst[:, :, 0:w], src[:, :, 0:w])
                            link(nc.vector.tensor_tensor(dst[:, :, w:T], src[:, :, w:T], src[:, :, 0:T - w], ALU.add))
                        shifted(pool_a, u2, 1)
                        shifted(pool_b, pool_a, 2)
                        shifted(pool_a[:, 1:2, :], pool_b[:, 1:2, :], 4)
                        nc.vector.tensor_copy(pool_a[64:128, 0:1, :], pool_b[64:128, 0:1, :])
                        shifted(pool_b[64:128, 1:2, :], pool_a[64:128, 1:2, :], 8)
                        link(nc.vector.tensor_copy(pool_a[64:128, 1:2, :], pool_b[64:128, 1:2, :]))
                        link(nc.vector.tensor_tensor(pool_b[:, :, 0:16], pool_a[:, :, 0:16],
                                                     pool_k[:, 0:32].rearrange("p (j t) -> p j t", j=2), ALU.mult))
                        for j in range(2):
                            link(nc.vector.scalar_tensor_tensor(pool_a[:, j, 16:T], pool_a[:, j, 16:T],
                                                                pool_k[:, 32 + j:33 + j], u2[:, j, 16:T], ALU.mult,
                                                                ALU.subtract))
                            link(nc.vector.tensor_tensor(u2[:, j, 0:16], pool_b[:, j, 0:16], u2[:, j, 0:16], ALU.subtract))
                            nc.vector.tensor_copy(u2[:, j, 16:T], pool_a[:, j, 16:T]).then_inc(S["pool_m"], 1)
                        ft = zt(15)[0:FOX_H, :]
                        fb = pc[0:FOX_H, R_FB + st.l:R_FB + st.l + 1]
                        link(nc.vector.tensor_scalar(ft, ft, fb, None, ALU.add))
                        link(nc.vector.tensor_scalar(fox_t[0], ft, -1.0, None, ALU.mult))
                        nc.vector.tensor_tensor(fox_t[1], fox_t[0], ft, ALU.min).then_inc(S["fox_a"], 1)
                        dve.wait_ge(S["fox_a"], st.at("fox_a", 1))
                        link(nc.vector.tensor_scalar(fox_t[0], ft, 0.0, None, ALU.min))
                        dve.wait_ge(S["fox_e"], st.at("fox_e", 2))
                        link(nc.vector.tensor_tensor(fox_t[0], fox_t[3], fox_t[0], ALU.subtract))
                        dve.wait_ge(S["rope_loaded"], 32)
                        nc.vector.tensor_tensor_scan(ft, rope[0:FOX_H, 0, :], fox_t[0], 0.0, ALU.mult, ALU.add
                                                     ).then_inc(S["fox_c"], 1)
                        for j in range(2):
                            dve.wait_ge(S["pool_y"], st.at("pool_y", j + 1))
                            r = R_PS + 2 * st.l + j
                            nc.vector.tensor_scalar(pool_tmps[j], bank(2 + j), pc[:, r:r + 1], None, ALU.mult
                                                    ).then_inc(S["pool_t"], 1)
                        for j in range(2):
                            dve.wait_ge(S["pool_hi"], st.at("pool_hi", j + 1))
                            low(hl_lat[:, 3 + j, :], pool_tmps[j], hh_lat[:, 3 + j, :]).then_inc(S["pool_lo"], 1)
                        for k in range(2):
                            dve.wait_ge(S["mla_root"], st.at("mla_root", k + 1))
                            link(nc.vector.reciprocal(mla_rs[k], mla_rs[k]))
                        for k in range(3):
                            r = R_QA + 2 * st.l + k if k < 2 else R_KVA + st.l
                            nc.vector.scalar_tensor_tensor(zt(k), zt(k), pc[:, r:r + 1], mla_rs[0 if k < 2 else 1],
                                                           ALU.mult, ALU.mult).then_inc(S["mla_n"], 1)
                        for i in range(1 + MLA_H):
                            x = zt(14)[64:96, :] if i == 0 else mla_qt[i - 1][64:96, :]
                            dve.wait_ge(S["mla_rot"], st.at("mla_rot", i + 1))
                            if i:
                                dve.wait_ge(S["mla_qf"], st.at("mla_qf", i))
                            link(nc.vector.tensor_tensor(mla_tb[64:96, :], bank(6)[64:96, :], rope[64:96, 1, :], ALU.mult))
                            link(nc.vector.tensor_tensor(x, x, rope[64:96, 0, :], ALU.mult))
                            nc.vector.tensor_tensor(x, x, mla_tb[64:96, :], ALU.add).then_inc(S["mla_qf"], 1)

            @block.gpsimd
            def _(pool):
                chain = [0]

                def link(ins):
                    chain[0] += 1
                    ins.then_inc(S["pool_chain"], 1)
                    pool.wait_ge(S["pool_chain"], chain[0])

                def sum_squares(m, sets, sq_sum=sq_sum, sq_tmp=sq_tmp):
                    for s in sets:
                        if m == 0:
                            o = nc.gpsimd.tensor_tensor(sq_sum[s], X[s][:, 0, :], X[s][:, 0, :], ALU.mult)
                            continue
                        link(nc.gpsimd.tensor_tensor(sq_tmp[s], X[s][:, m, :], X[s][:, m, :], ALU.mult))
                        o = nc.gpsimd.tensor_tensor(sq_sum[s], sq_sum[s], sq_tmp[s], ALU.add)
                    return o

                nc.gpsimd.memset(z[:, 6 * D:6 * D + P], 0.0).then_inc(S["rows_zero"], 1)
                nc.gpsimd.memset(marks[:, 3:4], 0.0).then_inc(S["z_taken"], 2)
                nc.gpsimd.memset(marks[:, 4:5], 0.0).then_inc(S["gate_taken"], 1)
                nc.gpsimd.memset(marks[:, 5:6], 0.0).then_inc(S["up_taken"], 1)
                nc.gpsimd.memset(marks[:, 6:7], 0.0).then_inc(S["silu_ready"], 1)
                nc.gpsimd.memset(marks[:, 7:8], 0.0).then_inc(S["h_lo"], 1)
                pool.wait_ge(S["x_copied"], 2 * (TT + CT))
                for m in range(KD):
                    o = sum_squares(m, ("lat", "ctx"))
                    if m < KD - 1:
                        link(o)
                o.then_inc(S["sumsq"], 1)
                for st in stages:
                    if st.kind == "linear_r" and st.final:
                        for m in range(KD):
                            pool.wait_ge(S["r_taken"], st.at("r_taken", m + 1))
                            if st.block2:
                                o = sum_squares(m, st.sets, {"lat": sq_sum2}, {"lat": sq_tmp2})
                            else:
                                o = sum_squares(m, st.sets)
                            if m < KD - 1:
                                link(o)
                        o.then_inc(S["sumsq"], 1)
                    elif st.kind == "mixer2":
                        pool.wait_ge(S["chunk_done"], st.chunk0 - 1)
                        nc.gpsimd.memset(pool_bd.rearrange("p j m -> p (j m)"), 0.0).then_inc(S["bd_zero"], 1)


_INS = ["x", "c", "ctx", "c_ctx", "w_mod", "b_mod", "norm1_g", "w_in", "q_norm_g", "k_norm_g", "gmlp_norm_g",
        "w_spatial", "b_spatial", "w_out", "norm2_g", "w_ff1", "w_ff2", "ffn1_norm_2", "ffn1_w_gu_2",
        "ffn1_w_down_2", "mix_norm_2", "w_in_2", "q_a_norm_2", "w_q_b_2", "kv_a_norm_2", "w_kv_b_2", "pool_w_2",
        "pool_scale_2", "fox_b_f_2", "w_out_2", "ffn2_norm_2", "ffn2_w_gu_2", "ffn2_w_down_2", "final_norm_2"]


def kernel(**inputs):
    import concourse.bacc as bacc
    from concourse.bass_utils import run_bass_kernel_spmd as run

    nc = bacc.Bacc("TRN2", target_bir_lowering=False, num_devices=1)
    arrays, args = {}, {}
    for name in _INS:
        arr = np.ascontiguousarray(inputs[name])
        arrays[f"in_{name}"] = arr
        args[name] = nc.dram_tensor(f"in_{name}", arr.shape, mybir.dt.from_np(arr.dtype), kind="ExternalInput").ap()
    arrays["consts"] = shape_constants()
    args["consts"] = nc.dram_tensor("consts", arrays["consts"].shape, F32, kind="ExternalInput").ap()
    out = nc.dram_tensor("out_0", (1, T, D), F32, kind="ExternalOutput").ap()
    build_program(nc, args, out)
    r = run(nc, [arrays], core_ids=[0])
    return r.results[0]["out_0"]
```
